# Optimizing a Trainium2 kernel written in Bass

```python
import math, functools
import jax, jax.numpy as jnp
from jax import lax
import numpy as np

D_MODEL = 1024
BATCH = 1
SEQ = 256
DEPTH = 1
DEC_BATCH = 8
DEC_SEQ = 1
PAST_LEN = 2048
PAGE_SIZE = 128

D_MIX = D_MODEL
D_ATTN = D_MIX // 2
D_CONV = D_MIX - D_ATTN
HEAD_DIM = 64
N_HEADS = D_ATTN // HEAD_DIM
CONV_W = 3
MOBA_BLOCK = 256
MOBA_TOPK = 3
D_FF = 2816
FFN_CONV_W = 3
Q_CHUNK = 16
LN_EPS = 1e-5
DEEPNORM_ALPHA = (2.0 * DEPTH) ** 0.25
DEEPNORM_BETA = (8.0 * DEPTH) ** -0.25
D_IN_PROJ = 3 * D_ATTN + 3 * D_CONV
SPLITS = (D_ATTN, 2 * D_ATTN, 3 * D_ATTN, 3 * D_ATTN + D_CONV, 3 * D_ATTN + 2 * D_CONV)

kernel_name = "hymba_moba_shortconv_convffn_deepnorm_step"

def alibi_slopes():
    return jnp.asarray(2.0 ** (-8.0 * np.arange(1, N_HEADS + 1) / N_HEADS), jnp.float32)

def layer_norm(x, g, b):
    xf = x.astype(jnp.float32)
    mu = jnp.mean(xf, axis=-1, keepdims=True)
    var = jnp.mean(jnp.square(xf - mu), axis=-1, keepdims=True)
    return ((xf - mu) * lax.rsqrt(var + LN_EPS) * g + b).astype(x.dtype)

def causal_dwconv(u, buf, w):
    t = u.shape[1]
    width = w.shape[0]
    ext = jnp.concatenate([buf.astype(u.dtype), u], axis=1)
    y = ext[:, 0:t] * w[0]
    for j in range(1, width):
        y = y + ext[:, j:j + t] * w[j]
    return y, ext[:, t:]

def moba_attend(q, t, kmean, fetch, slopes):
    nb = kmean.shape[1]
    k_sel = min(MOBA_TOPK, nb)
    own = t // MOBA_BLOCK
    gate = jnp.einsum('bthd,bnhd->bthn', q.astype(jnp.float32), kmean.astype(jnp.float32))
    past = jnp.arange(nb)[None, :] < own[:, None]
    gate = jnp.where(past[None, :, None, :], gate, -jnp.inf)
    _, sel = lax.top_k(gate, k_sel)
    n_past = jnp.minimum(own, MOBA_TOPK)
    sel_ok = jnp.arange(k_sel)[None, :] < n_past[:, None]
    one = sel.shape[:3] + (1,)
    blocks = jnp.concatenate([sel, jnp.broadcast_to(own[None, :, None, None], one)], axis=-1)
    ok = jnp.concatenate([jnp.broadcast_to(sel_ok[None, :, None, :], sel.shape),
                          jnp.ones(one, dtype=bool)], axis=-1)
    pos = blocks[..., None] * MOBA_BLOCK + jnp.arange(MOBA_BLOCK, dtype=blocks.dtype)
    valid = ok[..., None] & (pos <= t[None, :, None, None, None])
    pos = pos.reshape(pos.shape[:3] + (-1,))
    valid = valid.reshape(pos.shape)
    k_g, v_g = fetch(pos)
    s = jnp.einsum('bthd,bthnd->bthn', q, k_g, preferred_element_type=jnp.float32)
    s = s / math.sqrt(HEAD_DIM)
    dist = (t[None, :, None, None] - pos).astype(jnp.float32)
    s = s - slopes[None, None, :, None] * dist
    s = jnp.where(valid, s, -jnp.inf)
    p = jax.nn.softmax(s, axis=-1)
    return jnp.einsum('bthn,bthnd->bthd', p.astype(v_g.dtype), v_g)

def prompt_attend(q, k, v, slopes):
    bsz, s = q.shape[:2]
    nb = -(-s // MOBA_BLOCK)
    kpad = jnp.pad(k.astype(jnp.float32), ((0, 0), (0, nb * MOBA_BLOCK - s), (0, 0), (0, 0)))
    kmean = jnp.mean(kpad.reshape(bsz, nb, MOBA_BLOCK, N_HEADS, HEAD_DIM), axis=2)
    b_idx = jnp.arange(bsz)[:, None, None, None]
    h_idx = jnp.arange(N_HEADS)[None, None, :, None]

    def fetch(pos):
        pc = jnp.minimum(pos, s - 1)
        return k[b_idx, pc, h_idx], v[b_idx, pc, h_idx]

    nq = s // Q_CHUNK
    qc = q.reshape(bsz, nq, Q_CHUNK, N_HEADS, HEAD_DIM).transpose(1, 0, 2, 3, 4)
    tc = jnp.arange(s, dtype=jnp.int32).reshape(nq, Q_CHUNK)
    out = lax.map(lambda a: moba_attend(a[0], a[1], kmean, fetch, slopes), (qc, tc))
    return out.transpose(1, 0, 2, 3, 4).reshape(bsz, s, N_HEADS, HEAD_DIM)

def sample_attend(q, k, v, layer_idx, cache_k, cache_v, page_table, slopes):
    bsz, t = q.shape[:2]
    n_pages = PAST_LEN // PAGE_SIZE
    pages_per_block = MOBA_BLOCK // PAGE_SIZE
    total = PAST_LEN + t
    nb = -(-total // MOBA_BLOCK)
    pos_q = PAST_LEN + jnp.arange(t, dtype=jnp.int32)
    page_sum = jnp.sum(cache_k[layer_idx, page_table].astype(jnp.float32), axis=2)
    page_sum = jnp.pad(page_sum, ((0, 0), (0, nb * pages_per_block - n_pages), (0, 0), (0, 0)))
    page_sum = page_sum.at[:, pos_q // PAGE_SIZE].add(k.astype(jnp.float32))
    kmean = jnp.sum(page_sum.reshape(bsz, nb, pages_per_block, N_HEADS, HEAD_DIM), axis=2) / MOBA_BLOCK
    b_idx = jnp.arange(bsz)[:, None, None, None]
    h_idx = jnp.arange(N_HEADS)[None, None, :, None]

    def fetch(pos):
        is_past = (pos < PAST_LEN)[..., None]
        pp = jnp.clip(pos, 0, PAST_LEN - 1)
        page = page_table[b_idx, pp // PAGE_SIZE]
        off = pp % PAGE_SIZE
        pn = jnp.clip(pos - PAST_LEN, 0, t - 1)
        k_g = jnp.where(is_past, cache_k[layer_idx, page, off, h_idx].astype(k.dtype), k[b_idx, pn, h_idx])
        v_g = jnp.where(is_past, cache_v[layer_idx, page, off, h_idx].astype(v.dtype), v[b_idx, pn, h_idx])
        return k_g, v_g

    return moba_attend(q, pos_q, kmean, fetch, slopes)

def layer(x, attend, conv_buf, ffn_buf, w_in, w_conv, w_out, ln1_g, ln1_b,
          w_up, w_fconv, w_down, ln2_g, ln2_b):
    bsz, t = x.shape[:2]
    z = x @ w_in
    q, k, v, gb, gc, h = jnp.split(z, SPLITS, axis=-1)
    q = q.reshape(bsz, t, N_HEADS, HEAD_DIM)
    k = k.reshape(bsz, t, N_HEADS, HEAD_DIM)
    v = v.reshape(bsz, t, N_HEADS, HEAD_DIM)
    att = attend(q, k, v).reshape(bsz, t, D_ATTN)
    conv_y, conv_buf_new = causal_dwconv(gc * h, conv_buf, w_conv)
    mix = jnp.concatenate([att, gb * conv_y], axis=-1) @ w_out
    x1 = layer_norm(DEEPNORM_ALPHA * x + mix, ln1_g, ln1_b)
    up, ffn_buf_new = causal_dwconv(x1 @ w_up, ffn_buf, w_fconv)
    a, g = jnp.split(up, 2, axis=-1)
    f = (jax.nn.silu(a) * g) @ w_down
    y = layer_norm(DEEPNORM_ALPHA * x1 + f, ln2_g, ln2_b)
    return y, k, v, conv_buf_new, ffn_buf_new

def setup_inputs(seed: int = 0) -> dict:
    key = jax.random.key(seed)
    ks = jax.random.split(key, 20)
    n_pages = PAST_LEN // PAGE_SIZE
    n_phys = (DEC_BATCH * n_pages * 5) // 4
    f32 = jnp.float32
    x_prompt = jax.random.normal(ks[0], (BATCH, SEQ, D_MODEL), f32)
    x_sample = jax.random.normal(ks[1], (DEC_BATCH, DEC_SEQ, D_MODEL), f32)
    cache_k = jax.random.normal(ks[2], (DEPTH, n_phys, PAGE_SIZE, N_HEADS, HEAD_DIM), f32)
    cache_v = jax.random.normal(ks[3], (DEPTH, n_phys, PAGE_SIZE, N_HEADS, HEAD_DIM), f32) * DEEPNORM_BETA
    state_conv = jax.random.normal(ks[4], (DEPTH, DEC_BATCH, CONV_W - 1, D_CONV), f32)
    state_ffn_conv = jax.random.normal(ks[5], (DEPTH, DEC_BATCH, FFN_CONV_W - 1, 2 * D_FF), f32) * DEEPNORM_BETA
    page_table = jax.random.permutation(ks[6], n_phys)[:DEC_BATCH * n_pages].reshape(DEC_BATCH, n_pages).astype(jnp.int32)
    col_scale = jnp.concatenate([jnp.ones((2 * D_ATTN,), f32), jnp.full((D_ATTN,), DEEPNORM_BETA, f32),
                                 jnp.ones((3 * D_CONV,), f32)])
    w_in = jax.random.normal(ks[7], (DEPTH, D_MODEL, D_IN_PROJ), f32) * D_MODEL ** -0.5 * col_scale
    w_conv = jax.random.normal(ks[8], (DEPTH, CONV_W, D_CONV), f32) * CONV_W ** -0.5
    w_out = jax.random.normal(ks[9], (DEPTH, D_MIX, D_MODEL), f32) * D_MIX ** -0.5 * DEEPNORM_BETA
    ln1_g = 1.0 + 0.02 * jax.random.normal(ks[10], (DEPTH, D_MODEL), f32)
    ln1_b = 0.02 * jax.random.normal(ks[11], (DEPTH, D_MODEL), f32)
    w_ffn_up = jax.random.normal(ks[12], (DEPTH, D_MODEL, 2 * D_FF), f32) * D_MODEL ** -0.5 * DEEPNORM_BETA
    w_ffn_conv = jax.random.normal(ks[13], (DEPTH, FFN_CONV_W, 2 * D_FF), f32) * FFN_CONV_W ** -0.5
    w_ffn_down = jax.random.normal(ks[14], (DEPTH, D_FF, D_MODEL), f32) * D_FF ** -0.5 * DEEPNORM_BETA
    ln2_g = 1.0 + 0.02 * jax.random.normal(ks[15], (DEPTH, D_MODEL), f32)
    ln2_b = 0.02 * jax.random.normal(ks[16], (DEPTH, D_MODEL), f32)
    return {"x_prompt": x_prompt, "x_sample": x_sample, "cache_k": cache_k, "cache_v": cache_v,
            "state_conv": state_conv, "state_ffn_conv": state_ffn_conv, "page_table": page_table,
            "w_in": w_in, "w_conv": w_conv, "w_out": w_out, "ln1_g": ln1_g, "ln1_b": ln1_b,
            "w_ffn_up": w_ffn_up, "w_ffn_conv": w_ffn_conv, "w_ffn_down": w_ffn_down,
            "ln2_g": ln2_g, "ln2_b": ln2_b}

def reference(x_prompt, x_sample, cache_k, cache_v, state_conv, state_ffn_conv, page_table,
              w_in, w_conv, w_out, ln1_g, ln1_b, w_ffn_up, w_ffn_conv, w_ffn_down, ln2_g, ln2_b):
    slopes = alibi_slopes()
    bsz = x_prompt.shape[0]
    yp, ys = x_prompt, x_sample
    kp_l, vp_l, cp_l, fp_l, ks_l, vs_l, cs_l, fs_l = [], [], [], [], [], [], [], []
    for l in range(DEPTH):
        params = (w_in[l], w_conv[l], w_out[l], ln1_g[l], ln1_b[l],
                  w_ffn_up[l], w_ffn_conv[l], w_ffn_down[l], ln2_g[l], ln2_b[l])
        attend_p = functools.partial(prompt_attend, slopes=slopes)
        conv0 = jnp.zeros((bsz, CONV_W - 1, D_CONV), x_prompt.dtype)
        ffn0 = jnp.zeros((bsz, FFN_CONV_W - 1, 2 * D_FF), x_prompt.dtype)
        yp, kp, vp, cp, fp = layer(yp, attend_p, conv0, ffn0, *params)
        attend_s = functools.partial(sample_attend, layer_idx=l, cache_k=cache_k, cache_v=cache_v,
                                     page_table=page_table, slopes=slopes)
        ys, ks_, vs_, cs_, fs_ = layer(ys, attend_s, state_conv[l], state_ffn_conv[l], *params)
        kp_l.append(kp); vp_l.append(vp); cp_l.append(cp); fp_l.append(fp)
        ks_l.append(ks_); vs_l.append(vs_); cs_l.append(cs_); fs_l.append(fs_)
    k_prompt = jnp.stack(kp_l); v_prompt = jnp.stack(vp_l)
    conv_prompt = jnp.stack(cp_l); ffn_conv_prompt = jnp.stack(fp_l)
    k_sample = jnp.stack(ks_l); v_sample = jnp.stack(vs_l)
    conv_sample = jnp.stack(cs_l); ffn_conv_sample = jnp.stack(fs_l)
    return (yp, ys, k_prompt, v_prompt, conv_prompt, ffn_conv_prompt,
            k_sample, v_sample, conv_sample, ffn_conv_sample)


_drawn_inputs = setup_inputs


def setup_inputs(seed=0):
    import zlib

    import numpy as np

    out = dict(_drawn_inputs(seed))
    spreads = {}
    factors = {'ln1_g': 7.962, 'ln1_b': 7.743, 'ln2_g': 8.131, 'ln2_b': 8.153}
    for name, (base, spread) in spreads.items():
        noise = np.random.default_rng([zlib.crc32(name.encode()), seed]).standard_normal(out[name].shape)
        drawn = base * np.exp(spread * noise) if base else spread * noise
        out[name] = __import__('jax').numpy.asarray(drawn.astype(out[name].dtype))
    for name, factor in factors.items():
        out[name] = (out[name] * factor).astype(out[name].dtype)
    return out
```

```python
from contextlib import ExitStack

import numpy as np

import concourse.bass as bass
from concourse import mybir

ALU = mybir.AluOpType
ACT = mybir.ActivationFunctionType
AX = mybir.AxisListType
F32 = mybir.dt.float32
I32 = mybir.dt.int32

P = 128
D = 1024
KT = D // P
NPR = 256
NS = 8
R = NPR + NS
NH, DH = 8, 64
DA = NH * DH
NPAGE, PAGE = 16, 128
NBLK = 8
TOPK = 3
PAST = NPAGE * PAGE
FF = 2816
FT = FF // P
ALPHA = 2.0 ** 0.25
EPS = 1e-5
ZW = 2 + NPR + 3 * NS
UW = ZW - 2
TAIL = NPR - 2
NTAIL = R - TAIL
GP = 4
SLOTS = NPAGE // GP
FAR = 1.0e30
BIG = -1.0e30
STATE_ROWS = 2 * NS
STACK = STATE_ROWS + 3


def build(nc, x_prompt, x_sample, cache_k, cache_v, state_conv, state_ffn_conv, page_table,
          w_in, w_conv, w_out, ln1_g, ln1_b, w_ffn_up, w_ffn_conv, w_ffn_down, ln2_g, ln2_b,
          c_ident, c_dist, c_bias, c_slope, c_diag, c_head, c_tie, c_sel,
          y_prompt, y_sample, k_prompt, v_prompt, conv_prompt, ffn_conv_prompt,
          k_sample, v_sample, conv_sample, ffn_conv_sample):
    n_phys = cache_k.shape[1]
    pages_k = cache_k.rearrange("l n t h d -> (l n) t (h d)")
    pages_v = cache_v.rearrange("l n t h d -> (l n) t (h d)")
    win = w_in[0].rearrange("(k p) n -> p k n", p=P)
    wout = w_out[0].rearrange("(k p) n -> p k n", p=P)
    wup = w_ffn_up[0].rearrange("(k p) n -> p k n", p=P)
    wdown = w_ffn_down[0].rearrange("(k p) n -> p k n", p=P)

    ctx = ExitStack()
    with ctx:
        def sb(name, shape, dt=F32):
            return ctx.enter_context(nc.sbuf_tensor(name, shape, dt))[:]

        def sem(name):
            return ctx.enter_context(nc.semaphore(name))

        ident = sb("ident", [P, P])
        ones = sb("ones", [P, P])
        dist = sb("dist", [P, 3 * P])
        alibi = sb("alibi", [P, NPAGE, NH])
        slope = sb("slope", [P, NH])
        diag = sb("diag", [P, DA])
        headmask = sb("headmask", [P, 2])
        tie = sb("tie", [P, NBLK, NBLK], I32)
        pt = sb("pt", [1, NS * NPAGE], I32)
        xT = sb("xT", [P, KT, R])
        catT = sb("catT", [P, KT, R])
        rows = sb("rows", [P, 2, D])
        srows = sb("srows", [P, D])
        stT = sb("stT", [P, 48, STACK])
        lnr = sb("lnr", [16, P])
        lnT = sb("lnT", [P, 16])
        wring = sb("wring", [P, 2, KT * 512])
        KV = sb("KV", [P, SLOTS * GP * DA])
        zbuf = sb("zbuf", [P, 24 * R])
        qk = sb("qk", [P, 2, NS * DA])
        T = sb("T", [P, NS, NPAGE + 1, NH])
        gate = sb("gate", [P, NBLK, 4, NH])
        rank = sb("rank", [P, NBLK, 4, NH])
        smax = sb("smax", [P, 32])
        msum = sb("msum", [P, 32])
        rden = sb("rden", [P, 2, 32])
        m32 = sb("m32", [32, 1])
        dg32 = sb("dg32", [32, 32])
        qs = sb("qs", [P, DA])
        xsP = sb("xsP", [P, KT, 32])
        sel = sb("sel", [P, NS])
        qkT = sb("qkT", [P, 4, NS])
        ownT = sb("ownT", [P, 4 * NS, 2])
        Pw = sb("Pw", [P, 2, NPAGE + 1, 32])
        OM = sb("OM", [P, 2, DA])
        stage = sb("stage", [P, 2, NPR])
        vstage = sb("vstage", [P, 2, P])
        hs = sb("hs", [P, 2, 3 * P])
        hT = sb("hT", [P, 2, 3 * P])
        hst = sb("hst", [P, 2, 3, 2])
        hrec = sb("hrec", [P, 2, 2])
        cz = sb("cz", [P, ZW])
        cu = sb("cu", [P, UW])
        ct = sb("ct", [P, UW])
        ctail = sb("ctail", [NTAIL, DA])
        stats = sb("stats", [P, 3, 2, 6])
        mv = sb("mv", [P, 3, 2])
        rstd = sb("rstd", [P, 3])
        nhalf = sb("nhalf", [P, 1])

        stack = zbuf[0:STACK, 0:48 * P]
        zT = zbuf.rearrange("p (n r) -> p n r", r=R)
        kv = KV.rearrange("p (s g d) -> p s g d", s=SLOTS, g=GP)
        qb = qk[:, 0, :].rearrange("p (b d) -> p b d", b=NS)
        prod = qk[:, 1, :].rearrange("p (u n) -> p u n", u=2)
        cgt = qk[:, 1, 0:2048].rearrange("p (i m j) -> p i m j", i=NBLK, j=NBLK)
        cge = qk[:, 1, 2048:4096].rearrange("p (i m j) -> p i m j", i=NBLK, j=NBLK)
        wr_out = wring.rearrange("p s n -> p (s n)").rearrange("p (k n) -> p k n", k=KT)
        w2 = [KV[:, s * FT * P:(s + 1) * FT * P] for s in range(2)]
        Z = KV[:, 2 * FT * P:2 * FT * P + 4 * ZW].rearrange("p (s n) -> p s n", s=4)
        U = KV[:, 2 * FT * P + 4 * ZW:2 * FT * P + 8 * ZW].rearrange("p (s n) -> p s n", s=4)
        fT = zbuf[:, 0:FT * R].rearrange("p (n r) -> p n r", r=R)
        qflat = qk.rearrange("p a n -> p (a n)")
        x1T = qflat[:, 0:KT * R].rearrange("p (n r) -> p n r", r=R)
        rT = qflat[:, KT * R:2 * KT * R].rearrange("p (n r) -> p n r", r=R)
        g2 = qflat[:, 2 * KT * R:2 * KT * R + D]
        b2 = qflat[:, 2 * KT * R + D:2 * KT * R + 2 * D]
        uptail = qflat[:, 2 * KT * R + 2 * D:2 * KT * R + 2 * D + 44 * NTAIL].rearrange("p (n r) -> p n r", r=NTAIL)
        uprows = wring.rearrange("p s n -> p (s n)")[0:NTAIL, 0:2 * FF]

        ps = ctx.enter_context(nc.psum_tensor("ps", [P, 8, 512], F32))[:]

        s_id = sem("ident_landed")
        s_xs = sem("x_sample_landed")
        s_sel = sem("selector_landed")
        s_pad = sem("x_sample_padding")
        s_xsps, s_xsP = sem("x_sample_transposed"), sem("x_sample_copied")
        s_const = sem("const_landed")
        s_x = sem("x_landed")
        s_stack = sem("stack_landed")
        s_pt = sem("pages_landed")
        s_win = [sem(f"win_landed{i}") for i in range(2)]
        s_kv = [sem(f"kv_landed{i}") for i in range(SLOTS)]
        s_ones = sem("ones_set")
        s_zero = sem("padding_zeroed")
        s_xps = sem("x_transposed")
        s_xc = sem("x_copied")
        s_stps = sem("stack_transposed")
        s_std = sem("stack_copied")
        s_lnps, s_lnT = sem("ln_transposed"), sem("ln_copied")
        s_z = sem("z_product")
        s_ze = sem("z_copied")
        s_qsps, s_qs = sem("q_rows_ps"), sem("q_rows")
        s_qbps, s_qb = sem("q_broadcast_ps"), sem("q_broadcast")
        s_kused, s_vused = sem("k_slot_used"), sem("v_slot_used")
        s_red = sem("scores_summed")
        s_dve = sem("dve_chain")
        s_pool = sem("pool_chain")
        s_own, s_ownps, s_ownT = sem("own_products"), sem("own_ps"), sem("own_scores")
        s_gps = sem("gate_sums_ps")
        s_pm, s_pmps = sem("token_max"), sem("token_max_ps")
        s_dg, s_mps = sem("max_diag"), sem("max_broadcast_ps")
        s_sh, s_ex = sem("scores_shifted"), sem("probs_ready")
        s_sm, s_dps = sem("prob_sums"), sem("denominators_ps")
        s_soft = sem("denominators_inverted")
        s_rowps, s_rowcp = sem("kv_rows_ps"), sem("kv_rows_copied")
        s_ch, s_cvT = sem("mixer_gated"), sem("mixer_done")
        s_ctps, s_ctail = sem("mixer_tail_ps"), sem("mixer_tail")
        s_pw = sem("p_normalised")
        s_om = sem("pv_masked")
        s_ot, s_otc = sem("sample_out_ps"), sem("sample_out_copied")
        s_stg = sem("heads_staged")
        s_sc, s_scm = sem("head_scores"), sem("head_scores_masked")
        s_hm, s_nm, s_he = sem("head_raw_max"), sem("head_max"), sem("head_exp")
        s_hr, s_hp = sem("head_reciprocals"), sem("head_probs")
        s_htp, s_ht = sem("head_transposed"), sem("head_transposes_copied")
        s_ho, s_hoc = sem("head_out_ps"), sem("head_out_copied")
        s_wo = sem("w_out_landed")
        s_mix, s_r1 = sem("mix_product"), sem("residual1")
        s_var, s_rstd = sem("variances"), sem("inverse_deviations")
        s_n1, s_xh1 = sem("rows1_ps"), sem("rows1_normalised")
        s_b1, s_x1 = sem("x1_ps"), sem("x1_ready")
        s_wu = [sem(f"w_up_landed{i}") for i in range(2)]
        s_u, s_uz = sem("up_product"), sem("up_copied")
        s_zs = sem("up_states")
        s_c1 = sem("conv_steps")
        s_cv = sem("up_convolved")
        s_si = sem("silu_ready")
        s_f = sem("f_ready")
        s_utps, s_ut = sem("up_tail_ps"), sem("up_tail_rows")
        s_wd = [sem(f"w_down_landed{i}") for i in range(2)]
        s_dn, s_r2 = sem("down_product"), sem("residual2")
        s_n2, s_y = sem("rows2_ps"), sem("y_rows")
        s_g2 = sem("ln2_landed")
        s_kvo = sem("kv_rows_stored")
        s_out = sem("outputs_stored")

        def states(t, n):
            return t[:, n, 0:STATE_ROWS].rearrange("p (b k) -> p b k", k=2)

        def tap(t, n, k):
            return t[:, n, STATE_ROWS + k:STATE_ROWS + k + 1]

        def new_cols(z):
            return z[:, NPR + 4:ZW:3]

        block = ctx.enter_context(nc.Block())

        @block.sync
        def _(sp):
            sp.dma_start(ident, c_ident).then_inc(s_id, 16)
            sp.dma_start(srows[0:NS, :], x_sample.rearrange("b t d -> (b t) d")).then_inc(s_xs, 16)
            sp.dma_start(pt, page_table.rearrange("b n -> (b n)").rearrange("(o n) -> o n", o=1)).then_inc(s_pt, 16)
            sp.dma_start(sel, c_sel).then_inc(s_sel, 16)
            sp.wait_ge(s_pt, 16)

            def load(pages, b, s):
                _, ids = nc.values_load_multi_w_load_instructions(
                    pt[0:1, bass.ds(b * NPAGE + GP * s, GP)], engines=[mybir.EngineType.SP],
                    min_val=0, max_val=n_phys - 1)
                for g in range(GP):
                    sp.dma_start(kv[:, s, g, :],
                                 pages[bass.ds(ids[g], 1)].rearrange("o t d -> (o t) d")).then_inc(s_kv[s], 16)

            load(pages_k, 0, 0)
            sp.dma_start(rows, x_prompt[0].rearrange("(r p) d -> p r d", p=P)).then_inc(s_x, 16)
            load(pages_k, 0, 1)
            sp.dma_start(stack[0:STATE_ROWS, 0:2 * FF],
                         state_ffn_conv[0].rearrange("b k f -> (b k) f")).then_inc(s_stack, 16)
            sp.dma_start(stack[STATE_ROWS:STACK, 0:2 * FF], w_ffn_conv[0]).then_inc(s_stack, 16)
            sp.dma_start(stack[0:STATE_ROWS, 2 * FF:], state_conv[0].rearrange("b k f -> (b k) f")).then_inc(s_stack, 16)
            sp.dma_start(stack[STATE_ROWS:STACK, 2 * FF:], w_conv[0]).then_inc(s_stack, 16)
            for s in range(2, SLOTS):
                load(pages_k, 0, s)
            for dst, src in ((dist, c_dist), (alibi, c_bias), (slope, c_slope), (diag, c_diag),
                             (headmask, c_head), (tie, c_tie),
                             (lnr[0:8, :], ln1_g.rearrange("o (k p) -> (o k) p", p=P)),
                             (lnr[8:16, :], ln1_b.rearrange("o (k p) -> (o k) p", p=P))):
                sp.dma_start(dst, src).then_inc(s_const, 16)
            sp.dma_start(ffn_conv_sample[0, :, 0, :], state_ffn_conv[0, :, 1, :]).then_inc(s_out, 16)
            sp.dma_start(conv_sample[0, :, 0, :], state_conv[0, :, 1, :]).then_inc(s_out, 16)
            with sp.Fori(1, NS) as b:
                for s in range(SLOTS):
                    sp.wait_ge(s_kused, b * SLOTS + (s + 1 - SLOTS))
                    load(pages_k, b, s)
            for s in range(SLOTS):
                sp.wait_ge(s_kused, (NS - 1) * SLOTS + s + 1)
                load(pages_v, 0, s)
            with sp.Fori(1, NS) as b:
                for s in range(SLOTS):
                    sp.wait_ge(s_vused, b * SLOTS + (s + 1 - SLOTS))
                    load(pages_v, b, s)

            sp.wait_ge(s_rowcp, 6)
            kvr = rows.rearrange("p r (w d) -> p r w d", w=2)
            for w, (dst, dsts) in enumerate(((k_prompt, k_sample), (v_prompt, v_sample))):
                sp.dma_start(dst[0, 0].rearrange("(r p) h d -> p r (h d)", p=P), kvr[:, :, w, :]).then_inc(s_kvo, 16)
                sp.dma_start(dsts[0].rearrange("b t h d -> (b t) (h d)"),
                             srows[0:NS, w * DA:(w + 1) * DA]).then_inc(s_kvo, 16)
            sp.wait_ge(s_pw, 1)
            sp.dma_start(g2, ln2_g[0].partition_broadcast(P)).then_inc(s_g2, 16)
            sp.dma_start(b2, ln2_b[0].partition_broadcast(P)).then_inc(s_g2, 16)
            sp.wait_ge(s_ctail, 1)
            sp.dma_start(conv_prompt[0, 0], ctail[0:2, :]).then_inc(s_out, 16)
            sp.dma_start(conv_sample[0, :, 1, :], ctail[2:NTAIL, :]).then_inc(s_out, 16)

            def load_up(u, s):
                half = w2[s][:, 0:KT * 2 * P].rearrange("p (k a n) -> p k a n", k=KT, a=2)
                for a in range(2):
                    sp.dma_start(half[:, :, a, :], wup[:, :, bass.ds(u * P + a * FF, P)]).then_inc(s_wu[s], 16)

            sp.wait_ge(s_vused, NS * SLOTS)
            for s in range(2):
                load_up(s, s)
            with sp.Fori(1, FT // 2) as j:
                for s in range(2):
                    sp.wait_ge(s_u, 4 * j + (2 * s - 2))
                    load_up(2 * j + s, s)
            for s in range(2):
                sp.wait_ge(s_u, 2 * FT - 2 + 2 * s)
                sp.dma_start(w2[s].rearrange("p (k n) -> p k n", k=FT), wdown[:, :, s * P:(s + 1) * P]).then_inc(s_wd[s], 16)
            with sp.Fori(1, KT // 2) as j:
                for s in range(2):
                    sp.wait_ge(s_dn, 2 * j + (s - 1))
                    sp.dma_start(w2[s].rearrange("p (k n) -> p k n", k=FT),
                                 wdown[:, :, bass.ds(j * 2 * P + s * P, P)]).then_inc(s_wd[s], 16)
            sp.wait_ge(s_ut, 11)
            sp.dma_start(ffn_conv_prompt[0, 0], uprows[0:2, :]).then_inc(s_out, 16)
            sp.dma_start(ffn_conv_sample[0, :, 1, :], uprows[2:NTAIL, :]).then_inc(s_out, 16)
            yp = y_prompt[0].rearrange("(r p) d -> p r d", p=P)
            for r in range(2):
                sp.wait_ge(s_y, r + 1)
                sp.dma_start(yp[:, r, :], rows[:, r, :]).then_inc(s_out, 16)
            sp.wait_ge(s_y, 3)
            sp.dma_start(y_sample.rearrange("b t d -> (b t) d"), srows[0:NS, :]).then_inc(s_out, 16)
            sp.wait_ge(s_kvo, 16 * 4)
            sp.wait_ge(s_out, 16 * 9)

        @block.gpsimd
        def _(pool):
            steps = 0

            def chain(ins):
                nonlocal steps
                steps += 1
                ins.then_inc(s_pool, 1)
                pool.wait_ge(s_pool, steps)

            nc.gpsimd.memset(xsP, 0.0).then_inc(s_pad, 1)
            nc.gpsimd.memset(ones, 1.0).then_inc(s_ones, 1)
            nc.gpsimd.memset(nhalf, -0.5).then_inc(s_zero, 1)
            nc.gpsimd.memset(Pw, 0.0).then_inc(s_zero, 1)
            nc.gpsimd.memset(cz[:, 0:2], 0.0).then_inc(s_zero, 1)
            pool.wait_ge(s_zero, 3)
            pool.wait_ge(s_std, 2)
            for t in range(4):
                pool.wait_ge(s_ze, 20 + t + 1)
                nc.gpsimd.tensor_tensor(zT[:, 20 + t, :], zT[:, 16 + t, :], zT[:, 20 + t, :], ALU.mult).then_inc(s_ch, 1)
            pool.wait_ge(s_ch, 4)
            for t in range(4):
                chain(nc.gpsimd.tensor_copy(cz[:, 2:2 + NPR], zT[:, 20 + t, 0:NPR]))
                chain(nc.gpsimd.tensor_copy(new_cols(cz), zT[:, 20 + t, NPR:R]))
                zs = cz[:, 2 + NPR:ZW].rearrange("p (b k) -> p b k", k=3)
                chain(nc.gpsimd.tensor_copy(zs[:, :, 0:2], states(stT, 44 + t)))
                chain(nc.gpsimd.tensor_scalar(cu, cz[:, 2:ZW], tap(stT, 44 + t, 2), None, ALU.mult))
                for k in (1, 0):
                    chain(nc.gpsimd.tensor_scalar(ct, cz[:, k:k + UW], tap(stT, 44 + t, k), None, ALU.mult))
                    chain(nc.gpsimd.tensor_tensor(cu, cu, ct, ALU.add))
                chain(nc.gpsimd.tensor_tensor(catT[:, 4 + t, 0:NPR], cu[:, 0:NPR], zT[:, 12 + t, 0:NPR], ALU.mult))
                nc.gpsimd.tensor_tensor(catT[:, 4 + t, NPR:R], cu[:, NPR + 2:UW:3], zT[:, 12 + t, NPR:R],
                                        ALU.mult).then_inc(s_cvT, 1)
            pool.wait_ge(s_rowcp, 6)
            kvr = rows.rearrange("p r (w d) -> p r w d", w=2)
            with pool.Fori(0, 4) as t:
                nc.gpsimd.tensor_copy(stage[:, 0, :], zT[:, bass.ds(t, 1), 0:NPR].rearrange("p o n -> p (o n)")).then_inc(s_stg, 1)
                nc.gpsimd.tensor_copy(stage[:, 1, :], zT[:, bass.ds(t + 4, 1), 0:NPR].rearrange("p o n -> p (o n)")).then_inc(s_stg, 1)
                nc.gpsimd.tensor_copy(vstage, kvr[:, :, 1, bass.ds(t * P, P)]).then_inc(s_stg, 1)
                pool.wait_ge(s_ho, 2 * t + 2)
            pool.wait_ge(s_vused, NS * SLOTS)
            nc.gpsimd.memset(Z[:, :, 0:2], 0.0).then_inc(s_zs, 1)
            def deviations(first):
                for r in range(3):
                    n = P if r < 2 else NS
                    pool.wait_ge(s_var, first + r + 1)
                    chain(nc.gpsimd.tensor_scalar(mv[0:n, r, 1:2], mv[0:n, r, 1:2], EPS, None, ALU.add))
                    nc.gpsimd.tensor_tensor(rstd[0:n, r:r + 1], mv[0:n, r, 1:2], nhalf[0:n, :], ALU.pow).then_inc(s_rstd, 1)

            deviations(0)
            with pool.Fori(0, FT // 2) as j:
                for q in range(4):
                    pool.wait_ge(s_cv, 4 * j + (q + 1))
                    src = stT[:, bass.ds(2 * j + (q // 2 + q % 2 * FT), 1), 0:STATE_ROWS].rearrange("p o (b k) -> p (o b) k", k=2)
                    dst = Z[:, q, 2 + NPR:ZW].rearrange("p (b k) -> p b k", k=3)[:, :, 0:2]
                    nc.gpsimd.tensor_copy(dst, src).then_inc(s_zs, 1)
            deviations(3)

        @block.scalar
        def _(act):
            def load_win(c):
                act.dma_start(wring[:, c % 2, :].rearrange("p (k n) -> p k n", k=KT),
                              win[:, :, c * 512:(c + 1) * 512]).then_inc(s_win[c % 2], 16)

            load_win(0)
            for b in range(NS):
                if b == 2:
                    load_win(1)
                act.wait_ge(s_qbps, b + 1)
                nc.scalar.activation(qb[:, b, :], ps[:, 4 + b % 2, :], ACT.Copy).then_inc(s_qb, 1)
            act.wait_ge(s_stps, 1)
            nc.scalar.activation(stT[:, 0:24, :].rearrange("p n r -> p (n r)"), ps[:, 0, 0:24 * STACK], ACT.Copy).then_inc(s_std, 1)
            act.wait_ge(s_stps, 2)
            nc.scalar.activation(stT[:, 24:48, :].rearrange("p n r -> p (n r)"), ps[:, 1, 0:24 * STACK], ACT.Copy).then_inc(s_std, 1)
            for k in range(KT):
                act.wait_ge(s_xps, k + 1)
                nc.scalar.activation(xT[:, k, :], ps[:, (2 + k) % 4, 0:R], ACT.Copy).then_inc(s_xc, 1)

            def z_tile(n):
                act.wait_ge(s_z, n + 1)
                nc.scalar.activation(zT[:, n, :], ps[:, n % 4, 0:R], ACT.Copy).then_inc(s_ze, 1)

            for n in range(4):
                z_tile(n)
            for c in range(1, 6):
                if c + 1 < 6:
                    act.wait_ge(s_z, 4 * c)
                    load_win(c + 1)
                for n in range(4 * c, 4 * c + 4):
                    z_tile(n)
            act.wait_ge(s_z, 24)
            act.dma_start(wr_out, wout).then_inc(s_wo, 16)
            kvr = rows.rearrange("p r (w d) -> p r w d", w=2)
            for n in range(6):
                act.wait_ge(s_rowps, n + 1)
                if n < 4:
                    nc.scalar.activation(kvr[:, n // 2, n % 2, :], ps[:, n % 4, :], ACT.Copy).then_inc(s_rowcp, 1)
                else:
                    nc.scalar.activation(srows[0:NS, (n - 4) * DA:(n - 3) * DA], ps[0:NS, n % 4, :], ACT.Copy).then_inc(s_rowcp, 1)
            act.wait_ge(s_ownps, 1)
            own = T[:, :, NPAGE, :].rearrange("p b (t s) -> p t b s", s=2)
            for t in range(4):
                nc.scalar.activation(own[:, t], ps[:, 4, 16 * t:16 * t + 16].rearrange("p (b s) -> p b s", s=2),
                                     ACT.Copy).then_inc(s_ownT, 1)
            def exponentials(x):
                act.wait_ge(s_sh, x + 1)
                nc.scalar.activation(T[:, 4 * x:4 * x + 4], T[:, 4 * x:4 * x + 4], ACT.Exp, scale=0.125).then_inc(s_ex, 1)

            exponentials(0)
            act.wait_ge(s_ctps, 1)
            nc.scalar.activation(ctail, ps[0:NTAIL, 2, :], ACT.Copy).then_inc(s_ctail, 1)
            exponentials(1)
            act.sem_inc(s_otc, 1)
            with act.Fori(0, 4) as i:
                for s in range(2):
                    act.wait_ge(s_nm, 2 * i + s + 1)
                    for r, (a, b) in enumerate(((0, P), (P, 3 * P))):
                        nc.scalar.activation(hs[:, s, a:b], hs[:, s, a:b], ACT.Exp, bias=hst[:, s, 1, r:r + 1], scale=0.125,
                                             accum_out=hst[:, s, 2, r:r + 1]).then_inc(s_he, 1)
                for s in range(2):
                    act.wait_ge(s_htp, 2 * i + s + 1)
                    nc.scalar.activation(hT[:, s, :], ps[:, 1 + s, 0:3 * P], ACT.Copy).then_inc(s_ht, 1)
                act.wait_ge(s_ho, 2 * i + 2)
                nc.scalar.activation(catT[:, bass.ds(i, 1), 0:NPR].rearrange("p o n -> p (o n)"),
                                     ps[:, 3, 0:NPR], ACT.Copy).then_inc(s_hoc, 1)
                act.wait_ge(s_ot, i + 2)
                nc.scalar.activation(catT[:, 0:4, bass.ds(2 * i + NPR, 2)],
                                     ps[:, 0, 0:8].rearrange("p (t s) -> p t s", s=2), ACT.Copy).then_inc(s_otc, 1)
            for m in range(KT):
                act.wait_ge(s_b1, m + 1)
                nc.scalar.activation(x1T[:, m, :], ps[:, m % 4, 0:R], ACT.Identity, bias=lnT[:, 8 + m:9 + m],
                                     scale=lnT[:, m:m + 1]).then_inc(s_x1, 1)
            act.sem_inc(s_uz, 4)
            with act.Fori(0, FT // 2) as j:
                for s in range(2):
                    for a in range(2):
                        q = 2 * s + a
                        act.wait_ge(s_cv, 4 * j + (q + 1))
                        act.wait_ge(s_u, 4 * j + (q + 1))
                        bank = ps[:, q, :]
                        nc.scalar.activation(Z[:, q, 2:2 + NPR], bank[:, 0:NPR], ACT.Copy)
                        nc.scalar.activation(new_cols(Z[:, q, :]), bank[:, NPR:R], ACT.Copy)
                        nc.scalar.activation(uptail[:, bass.ds(2 * j + (s + a * FT), 1), :].rearrange("p o n -> p (o n)"),
                                             bank[:, TAIL:R], ACT.Copy).then_inc(s_uz, 1)
                    act.wait_ge(s_cv, 4 * j + (2 * s + 2 + 4))
                    nc.scalar.activation(U[:, 2 * s, 0:UW], U[:, 2 * s, 0:UW], ACT.Silu).then_inc(s_si, 1)
            for c in range(11):
                act.wait_ge(s_utps, c + 1)
                nc.scalar.activation(uprows[:, 512 * c:512 * c + 512], ps[0:NTAIL, 4 + c % 4, :], ACT.Copy).then_inc(s_ut, 1)

        @block.vector
        def _(dve):
            steps = 0

            def chain(ins):
                nonlocal steps
                steps += 1
                ins.then_inc(s_dve, 1)
                dve.wait_ge(s_dve, steps)

            dve.wait_ge(s_pad, 1)
            dve.wait_ge(s_xsps, 1)
            nc.vector.tensor_copy(xsP[:, :, 0:NS], ps[:, 6, 0:KT * NS].rearrange("p (k b) -> p k b", k=KT)).then_inc(s_xsP, 1)
            dve.wait_ge(s_qsps, 1)
            nc.vector.tensor_copy(qs, ps[:, 7, :]).then_inc(s_qs, 1)

            q4 = qb.rearrange("p b (o d) -> p b o d", o=1)

            def token_scores(first, end):
                with dve.Fori(first, end) as b:
                    dve.wait_ge(s_qb, b + 1)
                    q = q4[:, bass.ds(b, 1)].rearrange("p b o d -> p (b o) d").to_broadcast([P, GP, DA])
                    for s0 in (0, 2):
                        for s in (s0, s0 + 1):
                            dve.wait_ge(s_kv[s], 16 * GP * b + 16 * GP)
                            dve.wait_ge(s_red, SLOTS * b + (s + 1))
                            nc.vector.tensor_tensor(prod[:, s % 2, :].rearrange("p (g d) -> p g d", g=GP), kv[:, s], q,
                                                    ALU.mult).then_inc(s_kused, 1)
                        for s in (s0, s0 + 1):
                            dve.wait_ge(s_kused, SLOTS * b + (s + 1))
                            dst = T[:, bass.ds(b, 1), GP * s:GP * s + GP, :].rearrange("p o g h -> p (o g h)")
                            nc.vector.tensor_reduce(dst, prod[:, s % 2, :].rearrange("p (m d) -> p m d", d=DH), AX.X, ALU.add)\
                                .then_inc(s_red, 1)

            def softmax(x):
                Th = T[:, 4 * x:4 * x + 4]
                dve.wait_ge(s_gps, x + 1)
                for b in range(4):
                    src = ps[:, 4, P * b:P * b + P].rearrange("p (k two h) -> p k h two", two=2, h=NH)
                    last = nc.vector.tensor_reduce(gate[:, :, b, :], src, AX.X, ALU.add)
                chain(last)
                gflat = gate.rearrange("p k b h -> p k (b h)")
                gi = gflat.rearrange("p k (m o) -> p k m o", o=1).to_broadcast([P, NBLK, 32, NBLK])
                gj = gate.rearrange("p k b h -> p (b h) k").rearrange("p (o m) k -> p o m k", o=1)\
                    .to_broadcast([P, NBLK, 32, NBLK])
                nc.vector.tensor_tensor(cgt, gj, gi, ALU.is_gt)
                chain(nc.vector.tensor_tensor(cge, gj, gi, ALU.is_ge))
                tb = tie.rearrange("p i (o j) -> p i o j", o=1).to_broadcast([P, NBLK, 32, NBLK])
                chain(nc.vector.copy_predicated(cgt, tb, cge))
                chain(nc.vector.tensor_reduce(rank.rearrange("p k b h -> p k (b h)"), cgt, AX.X, ALU.add))
                chain(nc.vector.tensor_scalar(rank, rank, TOPK - 0.5, BIG, ALU.is_gt, ALU.mult))
                past = Th[:, :, 0:NPAGE, :].rearrange("p b g h -> p b (g h)")
                al = alibi.rearrange("p g h -> p (g h)").rearrange("p (o m) -> p o m", o=1).to_broadcast([P, 4, P])
                chain(nc.vector.tensor_tensor(past, past, al, ALU.add))
                for b in range(4):
                    pb = Th[:, b, 0:NPAGE, :].rearrange("p (k two) h -> p k two h", two=2)
                    rb = rank[:, :, b, :].rearrange("p k (o h) -> p k o h", o=1).to_broadcast([P, NBLK, 2, NH])
                    last = nc.vector.tensor_tensor(pb, pb, rb, ALU.add)
                if x == 0:
                    dve.wait_ge(s_ownT, 4)
                chain(last)
                nc.vector.tensor_reduce(smax.rearrange("p (b h) -> p b h", b=4), Th.rearrange("p b g h -> p b h g"),
                                        AX.X, ALU.max).then_inc(s_pm, 1)
                dve.wait_ge(s_pmps, x + 1)
                chain(nc.vector.tensor_reduce(m32, ps[0:32, 5, 0:P], AX.X, ALU.max))
                nc.vector.tensor_scalar(dg32, ident[0:32, 0:32], m32[:, 0:1], None, ALU.mult).then_inc(s_dg, 1)
                dve.wait_ge(s_mps, x + 1)
                mb = ps[:, 5, P:P + 32].rearrange("p (b o h) -> p b o h", b=4, o=1).to_broadcast([P, 4, NPAGE + 1, NH])
                nc.vector.tensor_tensor(Th, Th, mb, ALU.subtract).then_inc(s_sh, 1)
                dve.wait_ge(s_ex, x + 1)
                ow = Th[:, :, NPAGE, :]
                chain(nc.vector.tensor_tensor(ow, ow, ident[:, 4 * x:4 * x + 4].rearrange("p (b o) -> p b o", o=1)
                                              .to_broadcast([P, 4, NH]), ALU.mult))
                nc.vector.tensor_reduce(msum.rearrange("p (b h) -> p b h", b=4), Th.rearrange("p b g h -> p b h g"),
                                        AX.X, ALU.add).then_inc(s_sm, 1)
                dve.wait_ge(s_dps, x + 1)
                nc.vector.reciprocal(rden[:, x, :], ps[:, 5, 160:192]).then_inc(s_soft, 1)
                dve.wait_ge(s_soft, x + 1)

            dve.sem_inc(s_red, 2)
            token_scores(0, 3)
            dve.wait_ge(s_const, 16 * 8)
            dve.wait_ge(s_lnps, 1)
            nc.vector.tensor_copy(lnT, ps[:, 6, 0:16]).then_inc(s_lnT, 1)
            dve.wait_ge(s_ze, 8)
            chain(nc.vector.tensor_tensor(qkT, zT[:, 0:4, NPR:R], zT[:, 4:8, NPR:R], ALU.mult))
            nc.vector.tensor_tensor(
                ownT, qkT.rearrange("p t b -> p (t b)").rearrange("p (m o) -> p m o", o=1).to_broadcast([P, 32, 2]),
                headmask.rearrange("p (o s) -> p o s", o=1).to_broadcast([P, 32, 2]), ALU.mult).then_inc(s_own, 1)
            token_scores(3, 6)
            dve.wait_ge(s_red, 2 + 6 * SLOTS)
            softmax(0)
            token_scores(6, NS)

            rd = rden.rearrange("p x (b o h) -> p (x b) o h", b=4, o=1)
            dve.wait_ge(s_zero, 3)
            dve.sem_inc(s_om, 2)

            def sample_weights(i):
                for s in range(2):
                    nc.vector.tensor_tensor(Pw[:, s, :, 0:NH], T[:, bass.ds(2 * i + s, 1)].rearrange("p o g h -> p (o g) h"),
                                            rd[:, bass.ds(2 * i + s, 1)].rearrange("p b o h -> p (b o) h")
                                            .to_broadcast([P, NPAGE + 1, NH]), ALU.mult).then_inc(s_pw, 1)

            def masked_values(i, s):
                dve.wait_ge(s_vused, 8 * i + (4 * s + 4))
                nc.vector.tensor_tensor(OM[:, s, :], ps[:, 6 + s, :], diag, ALU.mult).then_inc(s_om, 1)

            def head_probabilities(i):
                for s in range(2):
                    dve.wait_ge(s_sc, 2 * i + (s + 1))
                    nc.vector.scalar_tensor_tensor(hs[:, s, :], dist, slope[:, bass.ds(2 * i + s, 1)], ps[:, 4 + s, 0:3 * P],
                                                   ALU.mult, ALU.add).then_inc(s_scm, 1)
                for s in range(2):
                    dve.wait_ge(s_scm, 2 * i + (s + 1))
                    for r, (a, b) in enumerate(((0, P), (P, 3 * P))):
                        last = nc.vector.tensor_reduce(hst[:, s, 0, r:r + 1], hs[:, s, a:b], AX.X, ALU.max)
                    last.then_inc(s_hm, 1)
                for s in range(2):
                    dve.wait_ge(s_hm, 2 * i + (s + 1))
                    nc.vector.tensor_scalar(hst[:, s, 1, :], hst[:, s, 0, :], -0.125, None, ALU.mult).then_inc(s_nm, 1)
                for s in range(2):
                    dve.wait_ge(s_he, 4 * i + (2 * s + 2))
                    nc.vector.reciprocal(hrec[:, s, :], hst[:, s, 2, :]).then_inc(s_hr, 1)
                for s in range(2):
                    dve.wait_ge(s_hr, 2 * i + (s + 1))
                    for r, (a, b) in enumerate(((0, P), (P, 3 * P))):
                        last = nc.vector.tensor_scalar(hs[:, s, a:b], hs[:, s, a:b], hrec[:, s, r:r + 1], None, ALU.mult)
                    last.then_inc(s_hp, 1)

            sample_weights(0)
            softmax(1)
            masked_values(0, 0)
            masked_values(0, 1)
            head_probabilities(0)
            with dve.Fori(1, 4) as i:
                sample_weights(i)
                dve.wait_ge(s_ot, i + 1)
                masked_values(i, 0)
                dve.wait_ge(s_htp, 2 * i)
                head_probabilities(i)
                masked_values(i, 1)

            def normalise(n, x, out, r, first):
                for c in range(2):
                    last = nc.vector.bn_stats(stats[0:n, r, c, :], x[:, c * 512:(c + 1) * 512])
                chain(last)
                nc.vector.bn_aggr(mv[0:n, r, :], stats[0:n, r, :, :]).then_inc(s_var, 1)
                dve.wait_ge(s_rstd, first + r + 1)
                return nc.vector.tensor_scalar(out, x, mv[0:n, r, 0:1], rstd[0:n, r:r + 1], ALU.subtract, ALU.mult)

            row_tiles = ((P, ps[:, 4:6, :], rows[:, 0, :]), (P, ps[:, 6:8, :], rows[:, 1, :]),
                         (NS, ps[0:NS, 2:4, :], srows[0:NS, :]))
            for m in range(KT):
                dve.wait_ge(s_mix, m + 1)
                nc.vector.scalar_tensor_tensor(rT[:, m, :], xT[:, m, :], ALPHA, ps[:, m % 4, 0:R], ALU.mult, ALU.add)\
                    .then_inc(s_r1, 1)
            dve.wait_ge(s_kvo, 64)
            for r, (n, x, out) in enumerate(row_tiles):
                dve.wait_ge(s_n1, r + 1)
                normalise(n, x.rearrange("p c n -> p (c n)"), out, r, 0).then_inc(s_xh1, 1)
            dve.sem_inc(s_cv, 4)
            with dve.Fori(0, FT // 2) as j:
                for s in range(2):
                    for a in range(2):
                        dve.wait_ge(s_zs, 4 * j + (2 * s + a + 2))
                        dve.wait_ge(s_uz, 4 * j + (2 * s + a + 1 + 4))
                    for k in (2, 1, 0):
                        for a in range(2):
                            q = 2 * s + a
                            w = stT[:, bass.ds(2 * j + (s + a * FT), 1), STATE_ROWS + k:STATE_ROWS + k + 1].rearrange("p o k -> p (o k)")
                            if k == 2:
                                ins = nc.vector.tensor_scalar(U[:, q, 0:UW], Z[:, q, 2:ZW], w, None, ALU.mult)
                            else:
                                dve.wait_ge(s_c1, 8 * j + (4 * s + 2 * (1 - k) + a + 1))
                                ins = nc.vector.scalar_tensor_tensor(U[:, q, 0:UW], Z[:, q, k:k + UW], w, U[:, q, 0:UW],
                                                                     ALU.mult, ALU.add)
                            ins.then_inc(s_c1 if k else s_cv, 1)
                for s in range(2):
                    dve.wait_ge(s_si, 2 * j + (s + 1))
                    fo = fT[:, bass.ds(2 * j + s, 1), :].rearrange("p o n -> p (o n)")
                    nc.vector.tensor_tensor(fo[:, 0:NPR], U[:, 2 * s, 0:NPR], U[:, 2 * s + 1, 0:NPR], ALU.mult)
                    nc.vector.tensor_tensor(fo[:, NPR:R], U[:, 2 * s, NPR + 2:UW:3], U[:, 2 * s + 1, NPR + 2:UW:3],
                                            ALU.mult).then_inc(s_f, 1)
                dve.wait_ge(s_f, 2 * j + 2)
            dve.sem_inc(s_r2, 2)
            with dve.Fori(0, KT // 2) as j:
                for s in range(2):
                    dve.wait_ge(s_dn, 2 * j + (s + 1))
                    nc.vector.scalar_tensor_tensor(rT[:, bass.ds(2 * j + s, 1), :].rearrange("p o n -> p (o n)"),
                                                   x1T[:, bass.ds(2 * j + s, 1), :].rearrange("p o n -> p (o n)"),
                                                   ALPHA, ps[:, s, 0:R], ALU.mult, ALU.add).then_inc(s_r2, 1)
            dve.wait_ge(s_g2, 32)
            for r, (n, x, out) in enumerate(row_tiles):
                dve.wait_ge(s_n2, r + 1)
                chain(normalise(n, x.rearrange("p c n -> p (c n)"), out, r, 3))
                chain(nc.vector.tensor_tensor(out, out, g2[0:n, :], ALU.mult))
                nc.vector.tensor_tensor(out, out, b2[0:n, :], ALU.add).then_inc(s_y, 1)

        @block.tensor
        def _(pe):
            def product(out, lhs, rhs, first=True, last=True):
                n = len(lhs)
                for k in range(n):
                    ins = nc.tensor.matmul(out, lhs[k], rhs[k], start=first and k == 0, stop=last and k == n - 1)
                return ins

            def turn(out, in_, n=P):
                return nc.tensor.transpose(out, in_, ident[0:n, 0:n])

            pe.wait_ge(s_id, 16)
            pe.wait_ge(s_xs, 16)
            for k in range(KT):
                ins = turn(ps[:, 6, k * NS:(k + 1) * NS], srows[0:NS, k * P:(k + 1) * P], NS)
            ins.then_inc(s_xsps, 1)
            pe.wait_ge(s_xsP, 1)
            pe.wait_ge(s_win[0], 16)
            w_q = wring[:, 0, :].rearrange("p (k n) -> p k n", k=KT)
            for k in range(KT):
                g = k % 4
                ins = nc.tensor.matmul(ps[32 * g:32 * g + 32, 7, :], xsP[:, k, :], w_q[:, k, :], start=k < 4, stop=k >= 4)
            ins.then_inc(s_qsps, 1)
            pe.wait_ge(s_qs, 1)
            pe.wait_ge(s_sel, 16)
            for b in range(NS):
                if b >= 2:
                    pe.wait_ge(s_qb, b - 1)
                nc.tensor.matmul(ps[:, 4 + b % 2, :], sel[:, b:b + 1].to_broadcast([P, P]), qs,
                                 start=True, stop=True).then_inc(s_qbps, 1)
            pe.wait_ge(s_stack, 64)
            for n in range(48):
                ins = turn(ps[:, n // 24, n % 24 * STACK:(n % 24 + 1) * STACK], stack[:, n * P:(n + 1) * P], STACK)
                if n % 24 == 23:
                    ins.then_inc(s_stps, 1)
            pe.wait_ge(s_x, 16)
            for k in range(KT):
                if k >= 4:
                    pe.wait_ge(s_xc, k - 3)
                elif k >= 2:
                    pe.wait_ge(s_std, k - 1)
                for r in range(2):
                    turn(ps[:, (2 + k) % 4, r * P:(r + 1) * P], rows[:, r, k * P:(k + 1) * P])
                turn(ps[:, (2 + k) % 4, NPR:R], srows[0:NS, k * P:(k + 1) * P], NS).then_inc(s_xps, 1)
            pe.wait_ge(s_xc, KT)

            x_tiles = [xT[:, k, :] for k in range(KT)]

            def chunk(c):
                w = wring[:, c % 2, :].rearrange("p (k n) -> p k n", k=KT)
                pe.wait_ge(s_win[c % 2], 16 * (c // 2 + 1))
                for i in range(4):
                    n = 4 * c + i
                    if n >= 4:
                        pe.wait_ge(s_ze, n - 3)
                    product(ps[:, n % 4, 0:R], [w[:, k, i * P:(i + 1) * P] for k in range(KT)], x_tiles).then_inc(s_z, 1)

            chunk(0)
            chunk(1)
            pe.wait_ge(s_const, 16 * 8)
            pe.wait_ge(s_xsP, 1)
            turn(ps[:, 6, 0:16], lnr, 16).then_inc(s_lnps, 1)
            for c in range(2, 6):
                chunk(c)
            for n in range(6):
                if n < 4:
                    pe.wait_ge(s_ze, 21 + n)
                else:
                    pe.wait_ge(s_rowcp, n - 3)
                cols = slice(n // 2 * P, n // 2 * P + P) if n < 4 else slice(NPR, R)
                m = P if n < 4 else NS
                for t in range(4):
                    ins = turn(ps[0:m, n % 4, t * P:(t + 1) * P], zT[:, 4 + 4 * (n % 2) + t, cols])
                ins.then_inc(s_rowps, 1)
            pe.wait_ge(s_ones, 1)
            pe.wait_ge(s_own, 1)
            pe.wait_ge(s_qb, NS)
            nc.tensor.matmul(ps[:, 4, 0:64], ones, ownT.rearrange("p m s -> p (m s)"), start=True, stop=True)\
                .then_inc(s_ownps, 1)
            pe.wait_ge(s_ownT, 4)

            def gate_sums(x):
                pe.wait_ge(s_red, 16 * (x + 1) + 2)
                nc.tensor.matmul(ps[:, 4, :], ones, T[:, 4 * x:4 * x + 4, 0:NPAGE, :].rearrange("p b g h -> p b (g h)"),
                                 start=True, stop=True).then_inc(s_gps, 1)

            def softmax_sums(x):
                pe.wait_ge(s_pm, x + 1)
                turn(ps[0:32, 5, 0:P], smax).then_inc(s_pmps, 1)
                pe.wait_ge(s_dg, x + 1)
                nc.tensor.matmul(ps[:, 5, P:P + 32], ones[0:32, :], dg32, start=True, stop=True).then_inc(s_mps, 1)
                pe.wait_ge(s_sm, x + 1)
                nc.tensor.matmul(ps[:, 5, 160:192], ones, msum, start=True, stop=True).then_inc(s_dps, 1)

            gate_sums(0)
            softmax_sums(0)
            pe.wait_ge(s_ch, 4)
            pe.wait_ge(s_rowcp, 3)
            for t in range(4):
                ins = turn(ps[0:NTAIL, 2, t * P:(t + 1) * P], zT[:, 20 + t, TAIL:R])
            ins.then_inc(s_ctps, 1)
            gate_sums(1)

            pe.wait_ge(s_ctail, 1)
            pe.wait_ge(s_rowcp, 6)
            pe.sem_inc(s_ot, 1)

            def values(i, s):
                pe.wait_ge(s_pw, 2 * i + (s + 1))
                pe.wait_ge(s_om, 2 * i + (s + 1))
                for sl in range(SLOTS):
                    pe.wait_ge(s_kv[sl], 32 * GP * i + 16 * GP * (NS + s + 1))
                    for g in range(GP):
                        ins = nc.tensor.matmul(ps[32 * g:32 * g + 32, 6 + s, :], Pw[:, s, GP * sl + g, :], kv[:, sl, g, :],
                                               start=sl == 0, stop=sl == SLOTS - 1 and g > 0)
                    if sl == SLOTS - 1:
                        ins = nc.tensor.matmul(ps[0:32, 6 + s, :], Pw[0:NS, s, NPAGE, :], srows[0:NS, DA:2 * DA],
                                               start=False, stop=True)
                    ins.then_inc(s_vused, 1)

            def head_scores(i):
                pe.wait_ge(s_stg, 3 * i + 3)
                for s in range(2):
                    h = slice(64 * s, 64 * s + 64)
                    nc.tensor.matmul(ps[:, 4 + s, 0:P], stage[h, 0, 0:P], stage[h, 1, 0:P], start=True, stop=True)
                    nc.tensor.matmul(ps[:, 4 + s, P:3 * P], stage[h, 0, P:NPR], stage[h, 1, :], start=True, stop=True)\
                        .then_inc(s_sc, 1)

            def outputs(i):
                for s in range(2):
                    pe.wait_ge(s_hp, 2 * i + (s + 1))
                    for n in range(3):
                        ins = turn(ps[:, 1 + s, n * P:(n + 1) * P], hs[:, s, n * P:(n + 1) * P])
                    ins.then_inc(s_htp, 1)
                for s in range(2):
                    pe.wait_ge(s_ht, 2 * i + (s + 1))
                    out = ps[64 * s:64 * s + 64, 3, 0:NPR]
                    v = [vstage[:, r, 64 * s:64 * s + 64] for r in range(2)]
                    nc.tensor.matmul(out, v[0], hT[:, s, 0:NPR], start=True, stop=False)
                    nc.tensor.matmul(out[:, P:NPR], v[1], hT[:, s, NPR:3 * P], start=False, stop=True).then_inc(s_ho, 1)
                pe.wait_ge(s_otc, i + 1)
                for s in range(2):
                    pe.wait_ge(s_om, 2 * i + (s + 1 + 2))
                    for t in range(4):
                        ins = nc.tensor.matmul(ps[:, 0, 2 * t + s:2 * t + s + 1], OM[:, s, t * P:(t + 1) * P], ones[:, 0:1],
                                               start=True, stop=True)
                ins.then_inc(s_ot, 1)

            values(0, 0)
            softmax_sums(1)
            values(0, 1)
            pe.wait_ge(s_soft, 2)
            head_scores(0)
            outputs(0)
            with pe.Fori(1, 4) as i:
                values(i, 0)
                pe.wait_ge(s_scm, 2 * i)
                head_scores(i)
                values(i, 1)
                pe.wait_ge(s_hoc, i)
                outputs(i)

            pe.wait_ge(s_wo, 16)
            pe.wait_ge(s_cvT, 4)
            pe.wait_ge(s_otc, 5)
            for m in range(KT):
                if m >= 4:
                    pe.wait_ge(s_r1, m - 3)
                product(ps[:, m % 4, 0:R], [wr_out[:, k, m * P:(m + 1) * P] for k in range(KT)],
                        [catT[:, k, :] for k in range(KT)]).then_inc(s_mix, 1)

            def to_rows(done):
                for bank, c0, n in ((4, 0, P), (6, P, P), (2, NPR, NS)):
                    for m in range(KT):
                        ins = turn(ps[0:n, bank + m // 4, m % 4 * P:(m % 4 + 1) * P], rT[:, m, c0:c0 + n])
                    ins.then_inc(done, 1)

            pe.wait_ge(s_r1, KT)
            to_rows(s_n1)
            for r in range(3):
                pe.wait_ge(s_xh1, r + 1)
            for m in range(KT):
                if m >= 4:
                    pe.wait_ge(s_x1, m - 3)
                for r in range(2):
                    turn(ps[:, m % 4, r * P:(r + 1) * P], rows[:, r, m * P:(m + 1) * P])
                turn(ps[:, m % 4, NPR:R], srows[0:NS, m * P:(m + 1) * P], NS).then_inc(s_b1, 1)

            pe.wait_ge(s_x1, KT)
            with pe.Fori(0, FT // 2) as j:
                for s in range(2):
                    w = w2[s][:, 0:KT * 2 * P].rearrange("p (k a n) -> p k a n", k=KT, a=2)
                    pe.wait_ge(s_wu[s], 32 * j + 32)
                    for a in range(2):
                        pe.wait_ge(s_uz, 4 * j + (2 * s + a + 1))
                        product(ps[:, 2 * s + a, 0:R], [w[:, k, a, :] for k in range(KT)],
                                [x1T[:, k, :] for k in range(KT)]).then_inc(s_u, 1)
            pe.wait_ge(s_uz, 4 + 2 * FT)
            for c in range(11):
                if c >= 4:
                    pe.wait_ge(s_ut, c - 3)
                for n in range(4 * c, 4 * c + 4):
                    ins = turn(ps[0:NTAIL, 4 + c % 4, n % 4 * P:(n % 4 + 1) * P], uptail[:, n, :])
                ins.then_inc(s_utps, 1)
            pe.wait_ge(s_f, FT)
            with pe.Fori(0, KT // 2) as j:
                for s in range(2):
                    w = w2[s].rearrange("p (k n) -> p k n", k=FT)
                    pe.wait_ge(s_wd[s], 16 * j + 16)
                    pe.wait_ge(s_r2, 2 * j + (s + 1))
                    product(ps[:, s, 0:R], [w[:, k, :] for k in range(FT)], [fT[:, k, :] for k in range(FT)]).then_inc(s_dn, 1)
            pe.wait_ge(s_r2, 2 + KT)
            pe.wait_ge(s_ut, 11)
            to_rows(s_n2)


def constants():
    h = np.arange(1, NH + 1, dtype=np.float64)
    sl = (-8.0 * 2.0 ** (-8.0 * h / NH)).astype(np.float32)
    tok = np.arange(P)
    past = PAST - (np.arange(NPAGE)[None, :] * PAGE + tok[:, None])
    k = np.arange(P)
    d00 = tok[:, None] - k[None, :]
    own = np.where(d00 >= 0, d00, FAR)
    diag = np.zeros((P, NH, DH), np.float32)
    for c in range(4):
        for i in range(NH):
            diag[32 * c + i, i] = 1.0
    tie = np.arange(NBLK)[None, :] < np.arange(NBLK)[:, None]
    pick = tok[:, None] % 32 == np.arange(NS)[None, :]
    head = (tok[:, None] // DH == np.arange(2)[None, :])
    return {
        "c_ident": np.eye(P, dtype=np.float32),
        "c_dist": np.concatenate([own, d00 + P, own], 1).astype(np.float32),
        "c_bias": (past[:, :, None] * sl[None, None, :]).astype(np.float32),
        "c_slope": np.ascontiguousarray(np.broadcast_to(sl, (P, NH))),
        "c_diag": diag.reshape(P, DA),
        "c_head": head.astype(np.float32),
        "c_tie": np.ascontiguousarray(np.broadcast_to(tie, (P, NBLK, NBLK)).astype(np.int32)),
        "c_sel": pick.astype(np.float32),
    }


_INS = ["x_prompt", "x_sample", "cache_k", "cache_v", "state_conv", "state_ffn_conv", "page_table",
        "w_in", "w_conv", "w_out", "ln1_g", "ln1_b", "w_ffn_up", "w_ffn_conv", "w_ffn_down", "ln2_g", "ln2_b"]
_OUTS = [(1, NPR, D), (NS, 1, D), (1, 1, NPR, NH, DH), (1, 1, NPR, NH, DH), (1, 1, 2, DA), (1, 1, 2, 2 * FF),
         (1, NS, 1, NH, DH), (1, NS, 1, NH, DH), (1, NS, 2, DA), (1, NS, 2, 2 * FF)]


def kernel(**inputs):
    import concourse.bacc as _bacc
    from concourse.bass_utils import run_bass_kernel_spmd as _run

    nc = _bacc.Bacc("TRN2", target_bir_lowering=False, num_devices=1)
    given = {n: np.ascontiguousarray(inputs[n]) for n in _INS}
    given.update(constants())
    arrays, args = {}, []
    for name, a in given.items():
        arrays[f"in_{name}"] = a
        args.append(nc.dram_tensor(f"in_{name}", a.shape, mybir.dt.from_np(a.dtype), kind="ExternalInput").ap())
    for i, shape in enumerate(_OUTS):
        args.append(nc.dram_tensor(f"out_{i}", shape, F32, kind="ExternalOutput").ap())
    build(nc, *args)
    r = _run(nc, [arrays], core_ids=[0])
    return tuple(r.results[0][f"out_{i}"] for i in range(len(_OUTS)))
```

```python
from contextlib import ExitStack

import numpy as np

import concourse.bass as bass
from concourse import mybir

ALU = mybir.AluOpType
ACT = mybir.ActivationFunctionType
AX = mybir.AxisListType
F32 = mybir.dt.float32
F32R = mybir.dt.float32r
I32 = mybir.dt.int32

P = 128
D = 1024
KT = D // P
NPR = 256
NS = 8
R = NPR + NS
NH, DH = 8, 64
DA = NH * DH
NPAGE, PAGE = 16, 128
NBLK = 8
TOPK = 3
PAST = NPAGE * PAGE
FF = 2816
FT = FF // P
ALPHA = 2.0 ** 0.25
EPS = 1e-5
ZW = 2 + NPR + 3 * NS
UW = ZW - 2
TAIL = NPR - 2
NTAIL = R - TAIL
GP = 4
SLOTS = NPAGE // GP
GD = GP - 1
FAR = 1.0e30
BIG = -1.0e30
STATE_ROWS = 2 * NS
STACK = STATE_ROWS + 3


def build(nc, x_prompt, x_sample, cache_k, cache_v, state_conv, state_ffn_conv, page_table,
          w_in, w_conv, w_out, ln1_g, ln1_b, w_ffn_up, w_ffn_conv, w_ffn_down, ln2_g, ln2_b,
          c_ident, c_dist, c_bias, c_slope, c_diag, c_head, c_tie, c_sel,
          y_prompt, y_sample, k_prompt, v_prompt, conv_prompt, ffn_conv_prompt,
          k_sample, v_sample, conv_sample, ffn_conv_sample):
    n_phys = cache_k.shape[1]
    pages_k = cache_k.rearrange("l n t h d -> (l n) t (h d)")
    pages_v = cache_v.rearrange("l n t h d -> (l n) t (h d)")
    win = w_in[0].rearrange("(k p) n -> p k n", p=P)
    wout = w_out[0].rearrange("(k p) n -> p k n", p=P)
    wup = w_ffn_up[0].rearrange("(k p) n -> p k n", p=P)
    wdown = w_ffn_down[0].rearrange("(k p) n -> p k n", p=P)

    ctx = ExitStack()
    with ctx:
        def sb(name, shape, dt=F32):
            return ctx.enter_context(nc.sbuf_tensor(name, shape, dt))[:]

        def sem(name):
            return ctx.enter_context(nc.semaphore(name))

        ident = sb("ident", [P, P])
        ones = sb("ones", [P, P])
        slope = sb("slope", [P, NH])
        diag = sb("diag", [P, DA])
        headmask = sb("headmask", [P, 2])
        tie = sb("tie", [P, NBLK, NBLK], I32)
        pt = sb("pt", [1, NS * NPAGE], I32)
        xT = sb("xT", [P, KT, R])
        catT = sb("catT", [P, KT, R])
        rows = sb("rows", [P, 2, D])
        srows = sb("srows", [P, D])
        stT = sb("stT", [P, 48, STACK])
        lnr = sb("lnr", [16, P])
        lnT = sb("lnT", [P, 16])
        xsP = sb("xsP", [P, KT, 32])
        attention_mem = nc.sbuf_base - KT * 32 * 4
        T = sb("T", [P, NS, NPAGE + 1, NH])
        gate = sb("gate", [P, NBLK, 4, NH])
        rank = sb("rank", [P, NBLK, 4, NH])
        qs = sb("qs", [P, DA])
        Pw = sb("Pw", [P, 2, NPAGE + 1, 32])
        OM = sb("OM", [P, 2, DA])
        stage = sb("stage", [P, 2, NPR])
        vstage = sb("vstage", [P, 2, P])
        hs = sb("hs", [P, 2, 3 * P])
        hT = sb("hT", [P, 2, 3 * P])
        cz = sb("cz", [P, ZW])
        cu = sb("cu", [P, UW])
        ct = sb("ct", [P, UW])
        alibi = sb("alibi", [P, NPAGE, NH])
        dist = sb("dist", [P, 3 * P])
        attention_end = nc.sbuf_base
        wring = sb("wring", [P, 2, KT * 512])
        wring_mem = nc.sbuf_base - 2 * KT * 512 * 4
        KV = sb("KV", [P, SLOTS * GP * DA])
        zbuf = sb("zbuf", [P, 24 * R])
        zbuf_mem = nc.sbuf_base - 24 * R * 4
        qk = sb("qk", [P, 2, NS * DA])
        qk_mem = nc.sbuf_base - 2 * NS * DA * 4
        smax = sb("smax", [P, 32])
        msum = sb("msum", [P, 32])
        rden = sb("rden", [P, 2, 32])
        m32 = sb("m32", [32, 1])
        dg32 = sb("dg32", [32, 32])
        sel = sb("sel", [P, NS])
        qkT = sb("qkT", [P, 4, NS])
        ownT = sb("ownT", [P, 4 * NS, 2])
        hst = sb("hst", [P, 2, 3, 2])
        hrec = sb("hrec", [P, 2, 2])
        ctail = sb("ctail", [NTAIL, DA])
        stats = sb("stats", [P, 3, 2, 6])
        mv = sb("mv", [P, 3, 2])
        rstd = sb("rstd", [P, 3])
        nhalf = sb("nhalf", [P, 1])

        stack = zbuf[0:STACK, 0:48 * P]
        zT = zbuf.rearrange("p (n r) -> p n r", r=R)
        kv = KV.rearrange("p (s g d) -> p s g d", s=SLOTS, g=GP)
        values_in = [wring.rearrange("p c (s g d) -> p (c s) g d", s=SLOTS // 2, g=GP), kv]
        qb = qk[:, 0, :].rearrange("p (b d) -> p b d", b=NS)
        prod = qk[:, 1, :].rearrange("p (u n) -> p u n", u=2)
        cgt = qk[:, 1, 0:2048].rearrange("p (i m j) -> p i m j", i=NBLK, j=NBLK)
        cge = qk[:, 1, 2048:4096].rearrange("p (i m j) -> p i m j", i=NBLK, j=NBLK)
        wr_out = qk.rearrange("p a n -> p (a n)").rearrange("p (k n) -> p k n", k=KT)
        w2 = [KV[:, s * FT * P:(s + 1) * FT * P] for s in range(2)]
        Z = KV[:, 2 * FT * P:2 * FT * P + 4 * ZW].rearrange("p (s n) -> p s n", s=4)
        U = KV[:, 2 * FT * P + 4 * ZW:2 * FT * P + 8 * ZW].rearrange("p (s n) -> p s n", s=4)
        uprows = sb("uprows", [2 * FT, NTAIL, P])

        def at(name, offset, shape):
            return nc.alloc_sbuf_tensor_at(name, shape, F32R, offset=offset)[:]

        unit = FT * P * 4
        whi = [at("whi0", wring_mem, [P, FT * P]), at("whi1", attention_mem, [P, FT * P])]
        wlo = [at("wlo0", wring_mem + unit, [P, FT * P]), at("wlo1", attention_mem + unit, [P, FT * P])]
        x1h = at("x1h", attention_mem + 2 * unit, [P, KT, R])
        assert attention_mem + 2 * unit + KT * R * 4 <= attention_end
        x1l = at("x1l", qk_mem + FT * R * 4, [P, KT, R])
        fh = at("fh", zbuf_mem, [P, FT, R])
        fl = at("fl", qk_mem, [P, FT, R])
        ftmp = sb("ftmp", [P, 2, R])
        rT = xT
        x1T = catT
        w_in_mem = wring.rearrange("p s n -> p (s n)")
        g2 = w_in_mem[:, 2 * FF:2 * FF + D]
        b2 = w_in_mem[:, 2 * FF + D:2 * FF + 2 * D]
        uptail = w_in_mem[:, 2 * FF + 2 * D:2 * FF + 2 * D + 2 * FT * NTAIL].rearrange("p (r n) -> p r n", r=NTAIL)

        ps = ctx.enter_context(nc.psum_tensor("ps", [P, 8, 512], F32))[:]

        s_id = sem("ident_landed")
        s_xs = sem("x_sample_landed")
        s_sel = sem("selector_landed")
        s_pad = sem("x_sample_padding")
        s_xsps, s_xsP = sem("x_sample_transposed"), sem("x_sample_copied")
        s_const = sem("const_landed")
        s_x = sem("x_landed")
        s_stack = sem("stack_landed")
        s_pt = sem("pages_landed")
        s_win = [sem(f"win_landed{i}") for i in range(2)]
        s_kv = [sem(f"kv_landed{i}") for i in range(SLOTS)]
        s_ve = [sem(f"even_v_landed{i}") for i in range(SLOTS)]
        s_ones = sem("ones_set")
        s_zero = sem("padding_zeroed")
        s_xps = sem("x_transposed")
        s_xc = sem("x_copied")
        s_stps = sem("stack_transposed")
        s_std = sem("stack_copied")
        s_lnps, s_lnT = sem("ln_transposed"), sem("ln_copied")
        s_z = sem("z_product")
        s_ze = sem("z_copied")
        s_qsps, s_qs = sem("q_rows_ps"), sem("q_rows")
        s_qbps, s_qb = sem("q_broadcast_ps"), sem("q_broadcast")
        s_kused, s_vused = sem("k_slot_used"), sem("v_slot_used")
        s_red, s_reda = sem("scores_summed_dve"), sem("scores_summed_act")
        s_dve = sem("dve_chain")
        s_pool = sem("pool_chain")
        s_own, s_ownps, s_ownT = sem("own_products"), sem("own_ps"), sem("own_scores")
        s_gps = sem("gate_sums_ps")
        s_pm, s_pmps = sem("token_max"), sem("token_max_ps")
        s_dg, s_mps = sem("max_diag"), sem("max_broadcast_ps")
        s_sh, s_ex = sem("scores_shifted"), sem("probs_ready")
        s_sm, s_dps = sem("prob_sums"), sem("denominators_ps")
        s_soft = sem("denominators_inverted")
        s_rowps, s_rowcp = sem("kv_rows_ps"), sem("kv_rows_copied")
        s_ch, s_cvT = sem("mixer_gated"), sem("mixer_done")
        s_ctps, s_ctail = sem("mixer_tail_ps"), sem("mixer_tail")
        s_pw = sem("p_normalised")
        s_om = sem("pv_masked")
        s_ot, s_otc = sem("sample_out_ps"), sem("sample_out_copied")
        s_stg = sem("heads_staged")
        s_sc, s_scm = sem("head_scores"), sem("head_scores_masked")
        s_hm, s_nm, s_he = sem("head_raw_max"), sem("head_max"), sem("head_exp")
        s_hr, s_hp = sem("head_reciprocals"), sem("head_probs")
        s_htp, s_ht = sem("head_transposed"), sem("head_transposes_copied")
        s_ho, s_hoc = sem("head_out_ps"), sem("head_out_copied")
        s_wo = sem("w_out_landed")
        s_mix, s_r1 = sem("mix_product"), sem("residual1")
        s_var, s_rstd = sem("variances"), sem("inverse_deviations")
        s_n1, s_xh1 = sem("rows1_ps"), sem("rows1_normalised")
        s_b1, s_x1 = sem("x1_ps"), sem("x1_ready")
        s_wu = [sem(f"w_up_landed{i}") for i in range(2)]
        s_hi, s_lo = sem("weights_high"), sem("weights_low")
        s_x1h, s_x1l = sem("x1_high"), sem("x1_low")
        s_fh, s_fs = sem("f_high"), sem("f_split")
        s_u, s_uz = sem("up_product"), sem("up_copied")
        s_zs = sem("up_states")
        s_c1 = sem("conv_steps")
        s_cv = sem("up_convolved")
        s_si = sem("silu_ready")
        s_f = sem("f_ready")
        s_utps, s_ut = sem("up_tail_ps"), sem("up_tail_rows")
        s_wd = [sem(f"w_down_landed{i}") for i in range(2)]
        s_dn, s_r2 = sem("down_product"), sem("residual2")
        s_n2, s_y = sem("rows2_ps"), sem("y_rows")
        s_g2 = sem("ln2_landed")
        s_kvo = sem("kv_rows_stored")
        s_out = sem("outputs_stored")

        def states(t, n):
            return t[:, n, 0:STATE_ROWS].rearrange("p (b k) -> p b k", k=2)

        def tap(t, n, k):
            return t[:, n, STATE_ROWS + k:STATE_ROWS + k + 1]

        def new_cols(z):
            return z[:, NPR + 4:ZW:3]

        block = ctx.enter_context(nc.Block())

        @block.sync
        def _(sp):
            sp.dma_start(ident, c_ident).then_inc(s_id, 16)
            sp.dma_start(srows[0:NS, :], x_sample.rearrange("b t d -> (b t) d")).then_inc(s_xs, 16)
            sp.dma_start(pt, page_table.rearrange("b n -> (b n)").rearrange("(o n) -> o n", o=1)).then_inc(s_pt, 16)
            sp.dma_start(sel, c_sel).then_inc(s_sel, 16)
            sp.wait_ge(s_pt, 16)

            def page_ids(b, first=0, n=NPAGE):
                return nc.values_load_multi_w_load_instructions(
                    pt[0:1, bass.ds(b * NPAGE + first, n)], engines=[mybir.EngineType.SP],
                    min_val=0, max_val=n_phys - 1)[1]

            def load(pages, ids, dst, landed):
                for g in range(GP):
                    sp.dma_start(dst[:, g, :], pages[bass.ds(ids[g], 1)].rearrange("o t d -> (o t) d")).then_inc(landed, 16)

            ids = page_ids(0, 0, GP)
            load(pages_k, ids, kv[:, 0], s_kv[0])
            sp.dma_start(rows, x_prompt[0].rearrange("(r p) d -> p r d", p=P)).then_inc(s_x, 16)
            ids = page_ids(0, GP, NPAGE - GP)
            load(pages_k, ids, kv[:, 1], s_kv[1])
            sp.dma_start(stack[0:STATE_ROWS, 0:2 * FF],
                         state_ffn_conv[0].rearrange("b k f -> (b k) f")).then_inc(s_stack, 16)
            sp.dma_start(stack[STATE_ROWS:STACK, 0:2 * FF], w_ffn_conv[0]).then_inc(s_stack, 16)
            sp.dma_start(stack[0:STATE_ROWS, 2 * FF:], state_conv[0].rearrange("b k f -> (b k) f")).then_inc(s_stack, 16)
            sp.dma_start(stack[STATE_ROWS:STACK, 2 * FF:], w_conv[0]).then_inc(s_stack, 16)
            for s in range(2, SLOTS):
                load(pages_k, ids[GP * (s - 1):], kv[:, s], s_kv[s])
            for dst, src in ((dist, c_dist), (alibi, c_bias), (slope, c_slope), (diag, c_diag),
                             (headmask, c_head), (tie, c_tie),
                             (lnr[0:8, :], ln1_g.rearrange("o (k p) -> (o k) p", p=P)),
                             (lnr[8:16, :], ln1_b.rearrange("o (k p) -> (o k) p", p=P))):
                sp.dma_start(dst, src).then_inc(s_const, 16)
            sp.dma_start(ffn_conv_sample[0, :, 0, :], state_ffn_conv[0, :, 1, :]).then_inc(s_out, 16)
            sp.dma_start(conv_sample[0, :, 0, :], state_conv[0, :, 1, :]).then_inc(s_out, 16)
            with sp.Fori(1, NS) as b:
                ids = page_ids(b)
                for s in range(SLOTS):
                    sp.wait_ge(s_kused, b * SLOTS + (s + 1 - SLOTS))
                    load(pages_k, ids[GP * s:], kv[:, s], s_kv[s])
            ids = page_ids(0)
            sp.wait_ge(s_z, 24)
            for s in range(SLOTS):
                load(pages_v, ids[GP * s:], values_in[0][:, s], s_ve[s])
            ids = page_ids(1)
            for s in range(SLOTS):
                sp.wait_ge(s_kused, (NS - 1) * SLOTS + s + 1)
                load(pages_v, ids[GP * s:], kv[:, s], s_kv[s])
            with sp.Fori(1, NS // 2) as i:
                for odd in range(2):
                    ids = page_ids(2 * i + odd)
                    for s in range(SLOTS):
                        sp.wait_ge(s_vused, 8 * i + (4 * odd + s + 1 - 8))
                        load(pages_v, ids[GP * s:], values_in[odd][:, s], (s_ve, s_kv)[odd][s])

            sp.wait_ge(s_rowcp, 6)
            kvr = rows.rearrange("p r (w d) -> p r w d", w=2)
            for w, (dst, dsts) in enumerate(((k_prompt, k_sample), (v_prompt, v_sample))):
                sp.dma_start(dst[0, 0].rearrange("(r p) h d -> p r (h d)", p=P), kvr[:, :, w, :]).then_inc(s_kvo, 16)
                sp.dma_start(dsts[0].rearrange("b t h d -> (b t) (h d)"),
                             srows[0:NS, w * DA:(w + 1) * DA]).then_inc(s_kvo, 16)
            sp.wait_ge(s_vused, NS * SLOTS)
            sp.dma_start(g2, ln2_g[0].partition_broadcast(P)).then_inc(s_g2, 16)
            sp.dma_start(b2, ln2_b[0].partition_broadcast(P)).then_inc(s_g2, 16)
            sp.wait_ge(s_ctail, 1)
            sp.dma_start(conv_prompt[0, 0], ctail[0:2, :]).then_inc(s_out, 16)
            sp.dma_start(conv_sample[0, :, 1, :], ctail[2:NTAIL, :]).then_inc(s_out, 16)

            def load_up(u, s):
                half = w2[s][:, 0:KT * 2 * P].rearrange("p (k a n) -> p k a n", k=KT, a=2)
                for a in range(2):
                    sp.dma_start(half[:, :, a, :], wup[:, :, bass.ds(u * P + a * FF, P)]).then_inc(s_wu[s], 16)

            sp.wait_ge(s_vused, NS * SLOTS)
            for s in range(2):
                load_up(s, s)
            with sp.Fori(1, FT // 2) as j:
                for s in range(2):
                    sp.wait_ge(s_lo, 2 * j + (s - 1))
                    load_up(2 * j + s, s)
            for s in range(2):
                sp.wait_ge(s_lo, FT - 1 + s)
                sp.dma_start(w2[s].rearrange("p (k n) -> p k n", k=FT), wdown[:, :, s * P:(s + 1) * P]).then_inc(s_wd[s], 16)
            with sp.Fori(1, KT // 2) as j:
                for s in range(2):
                    sp.wait_ge(s_lo, 2 * j + (FT + s - 1))
                    sp.dma_start(w2[s].rearrange("p (k n) -> p k n", k=FT),
                                 wdown[:, :, bass.ds(j * 2 * P + s * P, P)]).then_inc(s_wd[s], 16)
            sp.wait_ge(s_ut, 3)
            sp.dma_start(ffn_conv_prompt[0, 0].rearrange("r (n f) -> n r f", f=P), uprows[:, 0:2, :]).then_inc(s_out, 16)
            sp.dma_start(ffn_conv_sample[0, :, 1, :].rearrange("b (n f) -> n b f", f=P), uprows[:, 2:NTAIL, :]).then_inc(s_out, 16)
            yp = y_prompt[0].rearrange("(r p) d -> p r d", p=P)
            for r in range(2):
                sp.wait_ge(s_y, r + 1)
                sp.dma_start(yp[:, r, :], rows[:, r, :]).then_inc(s_out, 16)
            sp.wait_ge(s_y, 3)
            sp.dma_start(y_sample.rearrange("b t d -> (b t) d"), srows[0:NS, :]).then_inc(s_out, 16)
            sp.wait_ge(s_kvo, 16 * 4)
            sp.wait_ge(s_out, 16 * 9)

        @block.gpsimd
        def _(pool):
            steps = 0

            def chain(ins):
                nonlocal steps
                steps += 1
                ins.then_inc(s_pool, 1)
                pool.wait_ge(s_pool, steps)

            nc.gpsimd.memset(xsP, 0.0).then_inc(s_pad, 1)
            nc.gpsimd.memset(ones, 1.0).then_inc(s_ones, 1)
            nc.gpsimd.memset(nhalf, -0.5).then_inc(s_zero, 1)
            nc.gpsimd.memset(Pw, 0.0).then_inc(s_zero, 1)
            nc.gpsimd.memset(cz[:, 0:2], 0.0).then_inc(s_zero, 1)
            pool.wait_ge(s_zero, 3)
            pool.wait_ge(s_std, 2)
            for t in range(4):
                pool.wait_ge(s_ze, 20 + t + 1)
                nc.gpsimd.tensor_tensor(zT[:, 20 + t, :], zT[:, 16 + t, :], zT[:, 20 + t, :], ALU.mult).then_inc(s_ch, 1)
            pool.wait_ge(s_ch, 4)
            for t in range(4):
                chain(nc.gpsimd.tensor_copy(cz[:, 2:2 + NPR], zT[:, 20 + t, 0:NPR]))
                chain(nc.gpsimd.tensor_copy(new_cols(cz), zT[:, 20 + t, NPR:R]))
                zs = cz[:, 2 + NPR:ZW].rearrange("p (b k) -> p b k", k=3)
                chain(nc.gpsimd.tensor_copy(zs[:, :, 0:2], states(stT, 44 + t)))
                chain(nc.gpsimd.tensor_scalar(cu, cz[:, 2:ZW], tap(stT, 44 + t, 2), None, ALU.mult))
                for k in (1, 0):
                    chain(nc.gpsimd.tensor_scalar(ct, cz[:, k:k + UW], tap(stT, 44 + t, k), None, ALU.mult))
                    chain(nc.gpsimd.tensor_tensor(cu, cu, ct, ALU.add))
                chain(nc.gpsimd.tensor_tensor(catT[:, 4 + t, 0:NPR], cu[:, 0:NPR], zT[:, 12 + t, 0:NPR], ALU.mult))
                nc.gpsimd.tensor_tensor(catT[:, 4 + t, NPR:R], cu[:, NPR + 2:UW:3], zT[:, 12 + t, NPR:R],
                                        ALU.mult).then_inc(s_cvT, 1)
            pool.wait_ge(s_rowcp, 6)
            kvr = rows.rearrange("p r (w d) -> p r w d", w=2)
            with pool.Fori(0, 4) as t:
                nc.gpsimd.tensor_copy(stage[:, 0, :], zT[:, bass.ds(t, 1), 0:NPR].rearrange("p o n -> p (o n)")).then_inc(s_stg, 1)
                nc.gpsimd.tensor_copy(stage[:, 1, :], zT[:, bass.ds(t + 4, 1), 0:NPR].rearrange("p o n -> p (o n)")).then_inc(s_stg, 1)
                nc.gpsimd.tensor_copy(vstage, kvr[:, :, 1, bass.ds(t * P, P)]).then_inc(s_stg, 1)
                pool.wait_ge(s_ho, 2 * t + 2)
            pool.wait_ge(s_vused, NS * SLOTS)
            nc.gpsimd.memset(Z[:, :, 0:2], 0.0).then_inc(s_zs, 1)
            def deviations(first):
                for r in range(3):
                    n = P if r < 2 else NS
                    pool.wait_ge(s_var, first + r + 1)
                    chain(nc.gpsimd.tensor_scalar(mv[0:n, r, 1:2], mv[0:n, r, 1:2], EPS, None, ALU.add))
                    nc.gpsimd.tensor_tensor(rstd[0:n, r:r + 1], mv[0:n, r, 1:2], nhalf[0:n, :], ALU.pow).then_inc(s_rstd, 1)

            deviations(0)

            def unit_states(u, s):
                for a in range(2):
                    pool.wait_ge(s_cv, 2 * u + (a + 1))
                    src = stT[:, bass.ds(u + a * FT, 1), 0:STATE_ROWS].rearrange("p o (b k) -> p (o b) k", k=2)
                    dst = Z[:, 2 * s + a, 2 + NPR:ZW].rearrange("p (b k) -> p b k", k=3)[:, :, 0:2]
                    nc.gpsimd.tensor_copy(dst, src).then_inc(s_zs, 1)

            def split_f(u, s):
                pool.wait_ge(s_f, u + 1)
                ht = fh[:, bass.ds(u, 1), :].rearrange("p o n -> p (o n)")
                nc.gpsimd.tensor_copy(ht, ftmp[:, s, :]).then_inc(s_fh, 1)
                pool.wait_ge(s_fh, u + 1)
                nc.gpsimd.tensor_tensor(fl[:, bass.ds(u, 1), :].rearrange("p o n -> p (o n)"),
                                        ftmp[:, s, :], ht, ALU.subtract).then_inc(s_fs, 1)

            for s in range(2):
                unit_states(s, s)
            with pool.Fori(0, FT // 2 - 1) as j:
                for s in range(2):
                    split_f(2 * j + s, s)
                    unit_states(2 * j + (s + 2), s)
            for s in range(2):
                split_f(FT - 2 + s, s)
            deviations(3)

        @block.scalar
        def _(act):
            def load_win(c):
                act.dma_start(wring[:, c % 2, :].rearrange("p (k n) -> p k n", k=KT),
                              win[:, :, c * 512:(c + 1) * 512]).then_inc(s_win[c % 2], 16)

            load_win(0)
            for b in range(NS):
                if b == 2:
                    load_win(1)
                act.wait_ge(s_qbps, b + 1)
                nc.scalar.activation(qb[:, b, :], ps[:, 4 + b % 2, :], ACT.Copy).then_inc(s_qb, 1)
            def sum_products(b, s):
                act.wait_ge(s_kused, SLOTS * b + (s + 1))
                for g in range(GD, GP):
                    for h in range(NH):
                        x = prod[:, s % 2, g * DA + h * DH:g * DA + (h + 1) * DH]
                        dst = T[:, bass.ds(b, 1), GP * s + g, h:h + 1].rearrange("p o h -> p (o h)")
                        ins = nc.scalar.activation(x, x, ACT.Copy, accum_out=dst)
                ins.then_inc(s_reda, 1)

            sum_products(0, 0)
            sum_products(0, 1)
            act.wait_ge(s_stps, 1)
            nc.scalar.activation(stT[:, 0:24, :].rearrange("p n r -> p (n r)"), ps[:, 0, 0:24 * STACK], ACT.Copy).then_inc(s_std, 1)
            act.wait_ge(s_stps, 2)
            nc.scalar.activation(stT[:, 24:48, :].rearrange("p n r -> p (n r)"), ps[:, 1, 0:24 * STACK], ACT.Copy).then_inc(s_std, 1)
            for k in range(KT):
                act.wait_ge(s_xps, k + 1)
                nc.scalar.activation(xT[:, k, :], ps[:, (2 + k) % 4, 0:R], ACT.Copy).then_inc(s_xc, 1)

            def z_tile(n):
                act.wait_ge(s_z, n + 1)
                nc.scalar.activation(zT[:, n, :], ps[:, n % 4, 0:R], ACT.Copy).then_inc(s_ze, 1)

            sum_products(0, 2)
            sum_products(0, 3)
            for c in range(6):
                if c == 5:
                    act.wait_ge(s_ownps, 1)
                    own = T[:, :, NPAGE, :].rearrange("p b (t s) -> p t b s", s=2)
                    for t in range(4):
                        nc.scalar.activation(own[:, t], ps[:, 4, 16 * t:16 * t + 16].rearrange("p (b s) -> p b s", s=2),
                                             ACT.Copy).then_inc(s_ownT, 1)
                if 1 <= c < 5:
                    act.wait_ge(s_z, 4 * c)
                    load_win(c + 1)
                for i in range(4):
                    z_tile(4 * c + i)
                    sum_products(c + 1, i)
            kvr = rows.rearrange("p r (w d) -> p r w d", w=2)
            for n in range(6):
                act.wait_ge(s_rowps, n + 1)
                if n < 4:
                    nc.scalar.activation(kvr[:, n // 2, n % 2, :], ps[:, n % 4, :], ACT.Copy).then_inc(s_rowcp, 1)
                else:
                    nc.scalar.activation(srows[0:NS, (n - 4) * DA:(n - 3) * DA], ps[0:NS, n % 4, :], ACT.Copy).then_inc(s_rowcp, 1)
            def exponentials(x):
                act.wait_ge(s_sh, x + 1)
                nc.scalar.activation(T[:, 4 * x:4 * x + 4], T[:, 4 * x:4 * x + 4], ACT.Exp, scale=0.125).then_inc(s_ex, 1)

            exponentials(0)
            for i in range(SLOTS):
                sum_products(NS - 1, i)
            act.wait_ge(s_ctps, 1)
            nc.scalar.activation(ctail, ps[0:NTAIL, 2, :], ACT.Copy).then_inc(s_ctail, 1)
            exponentials(1)
            act.wait_ge(s_soft, 2)
            act.dma_start(wr_out, wout).then_inc(s_wo, 16)
            act.sem_inc(s_otc, 1)
            with act.Fori(0, 4) as i:
                for s in range(2):
                    act.wait_ge(s_nm, 2 * i + s + 1)
                    for r, (a, b) in enumerate(((0, P), (P, 3 * P))):
                        nc.scalar.activation(hs[:, s, a:b], hs[:, s, a:b], ACT.Exp, bias=hst[:, s, 1, r:r + 1], scale=0.125,
                                             accum_out=hst[:, s, 2, r:r + 1]).then_inc(s_he, 1)
                for s in range(2):
                    act.wait_ge(s_htp, 2 * i + s + 1)
                    nc.scalar.activation(hT[:, s, :], ps[:, 1 + s, 0:3 * P], ACT.Copy).then_inc(s_ht, 1)
                act.wait_ge(s_ho, 2 * i + 2)
                nc.scalar.activation(catT[:, bass.ds(i, 1), 0:NPR].rearrange("p o n -> p (o n)"),
                                     ps[:, 3, 0:NPR], ACT.Copy).then_inc(s_hoc, 1)
                act.wait_ge(s_ot, i + 2)
                nc.scalar.activation(catT[:, 0:4, bass.ds(2 * i + NPR, 2)],
                                     ps[:, 0, 0:8].rearrange("p (t s) -> p t s", s=2), ACT.Copy).then_inc(s_otc, 1)
            def up_high(u, s):
                act.wait_ge(s_wu[s], 16 * (u - s) + 32)
                nc.scalar.activation(whi[s][:, 0:KT * 2 * P], w2[s][:, 0:KT * 2 * P], ACT.Copy).then_inc(s_hi, 1)

            def down_high(m, s):
                act.wait_ge(s_wd[s], 8 * (m - s) + 16)
                nc.scalar.activation(whi[s], w2[s], ACT.Copy).then_inc(s_hi, 1)

            act.wait_ge(s_vused, NS * SLOTS)
            up_high(0, 0)
            up_high(1, 1)
            for m in range(KT):
                act.wait_ge(s_b1, m + 1)
                nc.scalar.activation(x1T[:, m, :], ps[:, 4 + m % 4, 0:R], ACT.Identity, bias=lnT[:, 8 + m:9 + m],
                                     scale=lnT[:, m:m + 1]).then_inc(s_x1, 1)
            act.sem_inc(s_uz, 4)

            def up_unit(u, s):
                for a in range(2):
                    q = 2 * s + a
                    act.wait_ge(s_cv, 2 * u + (a + 1))
                    act.wait_ge(s_u, 2 * u + (a + 1))
                    bank = ps[:, q, :]
                    nc.scalar.activation(Z[:, q, 2:2 + NPR], bank[:, 0:NPR], ACT.Copy)
                    nc.scalar.activation(new_cols(Z[:, q, :]), bank[:, NPR:R], ACT.Copy)
                    nc.scalar.activation(uptail[:, :, bass.ds(u + a * FT, 1)].rearrange("p n o -> p (n o)"),
                                         bank[:, TAIL:R], ACT.Copy).then_inc(s_uz, 1)

            def silu(u, s):
                act.wait_ge(s_cv, 2 * u + (2 + 4))
                nc.scalar.activation(U[:, 2 * s, 0:UW], U[:, 2 * s, 0:UW], ACT.Silu).then_inc(s_si, 1)

            def period(u, s, high, *unit):
                act.wait_ge(s_u, 2 * u + 2)
                high(*unit, s)
                silu(u - 1, 1 - s)
                up_unit(u, s)

            act.wait_ge(s_u, 2)
            up_high(2, 0)
            up_unit(0, 0)
            with act.Fori(0, FT // 2 - 2) as j:
                period(2 * j + 1, 1, up_high, 2 * j + 3)
                period(2 * j + 2, 0, up_high, 2 * j + 4)
            period(FT - 3, 1, up_high, FT - 1)
            period(FT - 2, 0, down_high, 0)
            period(FT - 1, 1, down_high, 1)
            silu(FT - 1, 1)
            for c in range(3):
                act.wait_ge(s_utps, c + 1)
                n = min(4, NTAIL - 4 * c)
                nc.scalar.activation(uprows[:, 4 * c:4 * c + n, :].rearrange("p r f -> p (r f)"),
                                     ps[0:2 * FT, 4 + c, 0:n * P], ACT.Copy).then_inc(s_ut, 1)
            with act.Fori(1, KT // 2) as j:
                for s in range(2):
                    act.wait_ge(s_dn, 2 * j + (s - 1))
                    down_high(2 * j + s, s)

        @block.vector
        def _(dve):
            steps = 0

            def chain(ins):
                nonlocal steps
                steps += 1
                ins.then_inc(s_dve, 1)
                dve.wait_ge(s_dve, steps)

            dve.wait_ge(s_pad, 1)
            dve.wait_ge(s_xsps, 1)
            nc.vector.tensor_copy(xsP[:, :, 0:NS], ps[:, 6, 0:KT * NS].rearrange("p (k b) -> p k b", k=KT)).then_inc(s_xsP, 1)
            dve.wait_ge(s_qsps, 1)
            nc.vector.tensor_copy(qs, ps[:, 7, :]).then_inc(s_qs, 1)

            q4 = qb.rearrange("p b (o d) -> p b o d", o=1)

            def token_scores(first, end):
                with dve.Fori(first, end) as b:
                    dve.wait_ge(s_qb, b + 1)
                    q = q4[:, bass.ds(b, 1)].rearrange("p b o d -> p (b o) d").to_broadcast([P, GP, DA])
                    for s0 in (0, 2):
                        for s in (s0, s0 + 1):
                            dve.wait_ge(s_kv[s], 16 * GP * b + 16 * GP)
                            dve.wait_ge(s_red, SLOTS * b + (s + 1))
                            dve.wait_ge(s_reda, SLOTS * b + (s + 1))
                            nc.vector.tensor_tensor(prod[:, s % 2, :].rearrange("p (g d) -> p g d", g=GP), kv[:, s], q,
                                                    ALU.mult).then_inc(s_kused, 1)
                        for s in (s0, s0 + 1):
                            dve.wait_ge(s_kused, SLOTS * b + (s + 1))
                            dst = T[:, bass.ds(b, 1), GP * s:GP * s + GD, :].rearrange("p o g h -> p (o g h)")
                            nc.vector.tensor_reduce(dst, prod[:, s % 2, 0:GD * DA].rearrange("p (m d) -> p m d", d=DH),
                                                    AX.X, ALU.add)\
                                .then_inc(s_red, 1)

            def softmax(x):
                Th = T[:, 4 * x:4 * x + 4]
                dve.wait_ge(s_gps, x + 1)
                for b in range(4):
                    src = ps[:, 4, P * b:P * b + P].rearrange("p (k two h) -> p k h two", two=2, h=NH)
                    last = nc.vector.tensor_reduce(gate[:, :, b, :], src, AX.X, ALU.add)
                chain(last)
                gflat = gate.rearrange("p k b h -> p k (b h)")
                gi = gflat.rearrange("p k (m o) -> p k m o", o=1).to_broadcast([P, NBLK, 32, NBLK])
                gj = gate.rearrange("p k b h -> p (b h) k").rearrange("p (o m) k -> p o m k", o=1)\
                    .to_broadcast([P, NBLK, 32, NBLK])
                nc.vector.tensor_tensor(cgt, gj, gi, ALU.is_gt)
                chain(nc.vector.tensor_tensor(cge, gj, gi, ALU.is_ge))
                tb = tie.rearrange("p i (o j) -> p i o j", o=1).to_broadcast([P, NBLK, 32, NBLK])
                chain(nc.vector.copy_predicated(cgt, tb, cge))
                chain(nc.vector.tensor_reduce(rank.rearrange("p k b h -> p k (b h)"), cgt, AX.X, ALU.add))
                chain(nc.vector.tensor_scalar(rank, rank, TOPK - 0.5, BIG, ALU.is_gt, ALU.mult))
                past = Th[:, :, 0:NPAGE, :].rearrange("p b g h -> p b (g h)")
                al = alibi.rearrange("p g h -> p (g h)").rearrange("p (o m) -> p o m", o=1).to_broadcast([P, 4, P])
                chain(nc.vector.tensor_tensor(past, past, al, ALU.add))
                for b in range(4):
                    pb = Th[:, b, 0:NPAGE, :].rearrange("p (k two) h -> p k two h", two=2)
                    rb = rank[:, :, b, :].rearrange("p k (o h) -> p k o h", o=1).to_broadcast([P, NBLK, 2, NH])
                    last = nc.vector.tensor_tensor(pb, pb, rb, ALU.add)
                if x == 0:
                    dve.wait_ge(s_ownT, 4)
                chain(last)
                nc.vector.tensor_reduce(smax.rearrange("p (b h) -> p b h", b=4), Th.rearrange("p b g h -> p b h g"),
                                        AX.X, ALU.max).then_inc(s_pm, 1)
                dve.wait_ge(s_pmps, x + 1)
                chain(nc.vector.tensor_reduce(m32, ps[0:32, 5, 0:P], AX.X, ALU.max))
                nc.vector.tensor_scalar(dg32, ident[0:32, 0:32], m32[:, 0:1], None, ALU.mult).then_inc(s_dg, 1)
                dve.wait_ge(s_mps, x + 1)
                mb = ps[:, 5, P:P + 32].rearrange("p (b o h) -> p b o h", b=4, o=1).to_broadcast([P, 4, NPAGE + 1, NH])
                nc.vector.tensor_tensor(Th, Th, mb, ALU.subtract).then_inc(s_sh, 1)
                dve.wait_ge(s_ex, x + 1)
                ow = Th[:, :, NPAGE, :]
                chain(nc.vector.tensor_tensor(ow, ow, ident[:, 4 * x:4 * x + 4].rearrange("p (b o) -> p b o", o=1)
                                              .to_broadcast([P, 4, NH]), ALU.mult))
                nc.vector.tensor_reduce(msum.rearrange("p (b h) -> p b h", b=4), Th.rearrange("p b g h -> p b h g"),
                                        AX.X, ALU.add).then_inc(s_sm, 1)
                dve.wait_ge(s_dps, x + 1)
                nc.vector.reciprocal(rden[:, x, :], ps[:, 5, 160:192]).then_inc(s_soft, 1)
                dve.wait_ge(s_soft, x + 1)

            dve.sem_inc(s_red, 2)
            dve.sem_inc(s_reda, 2)
            token_scores(0, 3)
            dve.wait_ge(s_const, 16 * 8)
            dve.wait_ge(s_lnps, 1)
            nc.vector.tensor_copy(lnT, ps[:, 6, 0:16]).then_inc(s_lnT, 1)
            dve.wait_ge(s_ze, 8)
            chain(nc.vector.tensor_tensor(qkT, zT[:, 0:4, NPR:R], zT[:, 4:8, NPR:R], ALU.mult))
            nc.vector.tensor_tensor(
                ownT, qkT.rearrange("p t b -> p (t b)").rearrange("p (m o) -> p m o", o=1).to_broadcast([P, 32, 2]),
                headmask.rearrange("p (o s) -> p o s", o=1).to_broadcast([P, 32, 2]), ALU.mult).then_inc(s_own, 1)
            token_scores(3, NS - 1)
            dve.wait_ge(s_red, 2 + (NS - 1) * SLOTS)
            dve.wait_ge(s_reda, 2 + (NS - 1) * SLOTS)
            softmax(0)
            token_scores(NS - 1, NS)
            dve.wait_ge(s_reda, 2 + NS * SLOTS)

            rd = rden.rearrange("p x (b o h) -> p (x b) o h", b=4, o=1)
            dve.wait_ge(s_zero, 3)
            dve.sem_inc(s_om, 2)

            def sample_weights(i):
                for s in range(2):
                    nc.vector.tensor_tensor(Pw[:, s, :, 0:NH], T[:, bass.ds(2 * i + s, 1)].rearrange("p o g h -> p (o g) h"),
                                            rd[:, bass.ds(2 * i + s, 1)].rearrange("p b o h -> p (b o) h")
                                            .to_broadcast([P, NPAGE + 1, NH]), ALU.mult).then_inc(s_pw, 1)

            def masked_values(i, s):
                dve.wait_ge(s_vused, 8 * i + (4 * s + 4))
                nc.vector.tensor_tensor(OM[:, s, :], ps[:, 6 + s, :], diag, ALU.mult).then_inc(s_om, 1)

            def head_probabilities(i):
                for s in range(2):
                    dve.wait_ge(s_sc, 2 * i + (s + 1))
                    nc.vector.scalar_tensor_tensor(hs[:, s, :], dist, slope[:, bass.ds(2 * i + s, 1)], ps[:, 4 + s, 0:3 * P],
                                                   ALU.mult, ALU.add).then_inc(s_scm, 1)
                for s in range(2):
                    dve.wait_ge(s_scm, 2 * i + (s + 1))
                    for r, (a, b) in enumerate(((0, P), (P, 3 * P))):
                        last = nc.vector.tensor_reduce(hst[:, s, 0, r:r + 1], hs[:, s, a:b], AX.X, ALU.max)
                    last.then_inc(s_hm, 1)
                for s in range(2):
                    dve.wait_ge(s_hm, 2 * i + (s + 1))
                    nc.vector.tensor_scalar(hst[:, s, 1, :], hst[:, s, 0, :], -0.125, None, ALU.mult).then_inc(s_nm, 1)
                for s in range(2):
                    dve.wait_ge(s_he, 4 * i + (2 * s + 2))
                    nc.vector.reciprocal(hrec[:, s, :], hst[:, s, 2, :]).then_inc(s_hr, 1)
                for s in range(2):
                    dve.wait_ge(s_hr, 2 * i + (s + 1))
                    for r, (a, b) in enumerate(((0, P), (P, 3 * P))):
                        last = nc.vector.tensor_scalar(hs[:, s, a:b], hs[:, s, a:b], hrec[:, s, r:r + 1], None, ALU.mult)
                    last.then_inc(s_hp, 1)

            sample_weights(0)
            softmax(1)
            masked_values(0, 0)
            masked_values(0, 1)
            head_probabilities(0)
            with dve.Fori(1, 4) as i:
                sample_weights(i)
                dve.wait_ge(s_ot, i + 1)
                masked_values(i, 0)
                dve.wait_ge(s_htp, 2 * i)
                head_probabilities(i)
                masked_values(i, 1)

            def normalise(n, x, out, r, first):
                for c in range(2):
                    last = nc.vector.bn_stats(stats[0:n, r, c, :], x[:, c * 512:(c + 1) * 512])
                chain(last)
                nc.vector.bn_aggr(mv[0:n, r, :], stats[0:n, r, :, :]).then_inc(s_var, 1)
                dve.wait_ge(s_rstd, first + r + 1)
                return nc.vector.tensor_scalar(out, x, mv[0:n, r, 0:1], rstd[0:n, r:r + 1], ALU.subtract, ALU.mult)

            row_tiles = ((P, ps[:, 4:6, :], rows[:, 0, :]), (P, ps[:, 6:8, :], rows[:, 1, :]),
                         (NS, ps[0:NS, 2:4, :], srows[0:NS, :]))
            def low(v, s, n):
                dve.wait_ge(s_hi, v + 1)
                nc.vector.tensor_tensor(wlo[s][:, 0:n], w2[s][:, 0:n], whi[s][:, 0:n], ALU.subtract).then_inc(s_lo, 1)

            for m in range(KT):
                if m >= 4 and m < 6:
                    low(m - 4, m - 4, KT * 2 * P)
                dve.wait_ge(s_mix, m + 1)
                nc.vector.scalar_tensor_tensor(rT[:, m, :], xT[:, m, :], ALPHA, ps[:, m % 4, 0:R], ALU.mult, ALU.add)\
                    .then_inc(s_r1, 1)
            dve.wait_ge(s_kvo, 64)
            for r, (n, x, out) in enumerate(row_tiles):
                dve.wait_ge(s_n1, r + 1)
                normalise(n, x.rearrange("p c n -> p (c n)"), out, r, 0).then_inc(s_xh1, 1)
            for m in range(KT):
                dve.wait_ge(s_x1, m + 1)
                nc.vector.tensor_copy(x1h[:, m, :], x1T[:, m, :]).then_inc(s_x1h, 1)
                dve.wait_ge(s_x1h, m + 1)
                nc.vector.tensor_tensor(x1l[:, m, :], x1T[:, m, :], x1h[:, m, :], ALU.subtract).then_inc(s_x1l, 1)

            dve.sem_inc(s_cv, 4)

            def up_unit(u, s):
                for a in range(2):
                    dve.wait_ge(s_zs, 2 * u + (a + 2))
                    dve.wait_ge(s_uz, 2 * u + (a + 1 + 4))
                for k in (2, 1, 0):
                    for a in range(2):
                        q = 2 * s + a
                        w = stT[:, bass.ds(u + a * FT, 1), STATE_ROWS + k:STATE_ROWS + k + 1].rearrange("p o k -> p (o k)")
                        if k == 2:
                            ins = nc.vector.tensor_scalar(U[:, q, 0:UW], Z[:, q, 2:ZW], w, None, ALU.mult)
                        else:
                            dve.wait_ge(s_c1, 4 * u + (2 * (1 - k) + a + 1))
                            ins = nc.vector.scalar_tensor_tensor(U[:, q, 0:UW], Z[:, q, k:k + UW], w, U[:, q, 0:UW],
                                                                 ALU.mult, ALU.add)
                        ins.then_inc(s_c1 if k else s_cv, 1)

            def gated(u, s):
                dve.wait_ge(s_si, u + 1)
                dve.wait_ge(s_fs, u + 1)
                nc.vector.tensor_tensor(ftmp[:, s, 0:NPR], U[:, 2 * s, 0:NPR], U[:, 2 * s + 1, 0:NPR], ALU.mult)
                nc.vector.tensor_tensor(ftmp[:, s, NPR:R], U[:, 2 * s, NPR + 2:UW:3], U[:, 2 * s + 1, NPR + 2:UW:3],
                                        ALU.mult).then_inc(s_f, 1)

            dve.sem_inc(s_fs, 2)

            def period(u, s, v, n):
                low(v, s, n)
                gated(u - 1, 1 - s)
                up_unit(u, s)

            low(2, 0, KT * 2 * P)
            up_unit(0, 0)
            with dve.Fori(0, FT // 2 - 2) as j:
                period(2 * j + 1, 1, 2 * j + 3, KT * 2 * P)
                period(2 * j + 2, 0, 2 * j + 4, KT * 2 * P)
            period(FT - 3, 1, FT - 1, KT * 2 * P)
            period(FT - 2, 0, FT, FT * P)
            gated(FT - 2, 0)
            up_unit(FT - 1, 1)
            gated(FT - 1, 1)
            low(FT + 1, 1, FT * P)
            dve.sem_inc(s_r2, 2)

            def second_residual(m, s):
                dve.wait_ge(s_dn, m + 1)
                nc.vector.scalar_tensor_tensor(rT[:, bass.ds(m, 1), :].rearrange("p o n -> p (o n)"),
                                               x1T[:, bass.ds(m, 1), :].rearrange("p o n -> p (o n)"),
                                               ALPHA, ps[:, s, 0:R], ALU.mult, ALU.add).then_inc(s_r2, 1)

            with dve.Fori(0, KT // 2 - 1) as j:
                for s in range(2):
                    low(2 * j + (FT + s + 2), s, FT * P)
                    second_residual(2 * j + s, s)
            for s in range(2):
                second_residual(KT - 2 + s, s)
            dve.wait_ge(s_g2, 32)
            for r, (n, x, out) in enumerate(row_tiles):
                dve.wait_ge(s_n2, r + 1)
                chain(normalise(n, x.rearrange("p c n -> p (c n)"), out, r, 3))
                chain(nc.vector.tensor_tensor(out, out, g2[0:n, :], ALU.mult))
                nc.vector.tensor_tensor(out, out, b2[0:n, :], ALU.add).then_inc(s_y, 1)

        @block.tensor
        def _(pe):
            def product(out, lhs, rhs, first=True, last=True):
                n = len(lhs)
                for k in range(n):
                    ins = nc.tensor.matmul(out, lhs[k], rhs[k], start=first and k == 0, stop=last and k == n - 1)
                return ins

            def turn(out, in_, n=P):
                return nc.tensor.transpose(out, in_, ident[0:n, 0:n])

            pe.wait_ge(s_id, 16)
            pe.wait_ge(s_xs, 16)
            for k in range(KT):
                ins = turn(ps[:, 6, k * NS:(k + 1) * NS], srows[0:NS, k * P:(k + 1) * P], NS)
            ins.then_inc(s_xsps, 1)
            pe.wait_ge(s_xsP, 1)
            pe.wait_ge(s_win[0], 16)
            w_q = wring[:, 0, :].rearrange("p (k n) -> p k n", k=KT)
            for k in range(KT):
                g = k % 4
                ins = nc.tensor.matmul(ps[32 * g:32 * g + 32, 7, :], xsP[:, k, :], w_q[:, k, :], start=k < 4, stop=k >= 4)
            ins.then_inc(s_qsps, 1)
            pe.wait_ge(s_qs, 1)
            pe.wait_ge(s_sel, 16)
            for b in range(NS):
                if b >= 2:
                    pe.wait_ge(s_qb, b - 1)
                nc.tensor.matmul(ps[:, 4 + b % 2, :], sel[:, b:b + 1].to_broadcast([P, P]), qs,
                                 start=True, stop=True).then_inc(s_qbps, 1)
            pe.wait_ge(s_stack, 64)
            for n in range(48):
                ins = turn(ps[:, n // 24, n % 24 * STACK:(n % 24 + 1) * STACK], stack[:, n * P:(n + 1) * P], STACK)
                if n % 24 == 23:
                    ins.then_inc(s_stps, 1)
            pe.wait_ge(s_x, 16)
            for k in range(KT):
                if k >= 4:
                    pe.wait_ge(s_xc, k - 3)
                elif k >= 2:
                    pe.wait_ge(s_std, k - 1)
                for r in range(2):
                    turn(ps[:, (2 + k) % 4, r * P:(r + 1) * P], rows[:, r, k * P:(k + 1) * P])
                turn(ps[:, (2 + k) % 4, NPR:R], srows[0:NS, k * P:(k + 1) * P], NS).then_inc(s_xps, 1)
            pe.wait_ge(s_xc, KT)

            x_tiles = [xT[:, k, :] for k in range(KT)]

            def chunk(c):
                w = wring[:, c % 2, :].rearrange("p (k n) -> p k n", k=KT)
                pe.wait_ge(s_win[c % 2], 16 * (c // 2 + 1))
                for i in range(4):
                    n = 4 * c + i
                    if n >= 4:
                        pe.wait_ge(s_ze, n - 3)
                    product(ps[:, n % 4, 0:R], [w[:, k, i * P:(i + 1) * P] for k in range(KT)], x_tiles).then_inc(s_z, 1)

            chunk(0)
            chunk(1)
            pe.wait_ge(s_const, 16 * 8)
            pe.wait_ge(s_xsP, 1)
            turn(ps[:, 6, 0:16], lnr, 16).then_inc(s_lnps, 1)
            for c in range(2, 5):
                chunk(c)
            pe.wait_ge(s_ones, 1)
            pe.wait_ge(s_own, 1)
            pe.wait_ge(s_qb, NS)
            nc.tensor.matmul(ps[:, 4, 0:64], ones, ownT.rearrange("p m s -> p (m s)"), start=True, stop=True)\
                .then_inc(s_ownps, 1)
            chunk(5)
            for n in range(6):
                if n < 4:
                    pe.wait_ge(s_ze, 21 + n)
                else:
                    pe.wait_ge(s_rowcp, n - 3)
                cols = slice(n // 2 * P, n // 2 * P + P) if n < 4 else slice(NPR, R)
                m = P if n < 4 else NS
                for t in range(4):
                    ins = turn(ps[0:m, n % 4, t * P:(t + 1) * P], zT[:, 4 + 4 * (n % 2) + t, cols])
                ins.then_inc(s_rowps, 1)
            def gate_sums(x):
                pe.wait_ge(s_ownT, 4)
                pe.wait_ge(s_red, 16 * (x + 1) + 2)
                pe.wait_ge(s_reda, 16 * (x + 1) + 2)
                nc.tensor.matmul(ps[:, 4, :], ones, T[:, 4 * x:4 * x + 4, 0:NPAGE, :].rearrange("p b g h -> p b (g h)"),
                                 start=True, stop=True).then_inc(s_gps, 1)

            def softmax_sums(x):
                pe.wait_ge(s_pm, x + 1)
                turn(ps[0:32, 5, 0:P], smax).then_inc(s_pmps, 1)
                pe.wait_ge(s_dg, x + 1)
                nc.tensor.matmul(ps[:, 5, P:P + 32], ones[0:32, :], dg32, start=True, stop=True).then_inc(s_mps, 1)
                pe.wait_ge(s_sm, x + 1)
                nc.tensor.matmul(ps[:, 5, 160:192], ones, msum, start=True, stop=True).then_inc(s_dps, 1)

            gate_sums(0)
            softmax_sums(0)
            pe.wait_ge(s_ch, 4)
            pe.wait_ge(s_rowcp, 3)
            for t in range(4):
                ins = turn(ps[0:NTAIL, 2, t * P:(t + 1) * P], zT[:, 20 + t, TAIL:R])
            ins.then_inc(s_ctps, 1)
            gate_sums(1)

            pe.wait_ge(s_ctail, 1)
            pe.wait_ge(s_rowcp, 6)
            pe.sem_inc(s_ot, 1)

            def values(i, s):
                pe.wait_ge(s_pw, 2 * i + (s + 1))
                pe.wait_ge(s_om, 2 * i + (s + 1))
                for sl in range(SLOTS):
                    if s == 0:
                        pe.wait_ge(s_ve[sl], 16 * GP * i + 16 * GP)
                    else:
                        pe.wait_ge(s_kv[sl], 16 * GP * i + 16 * GP * (NS + 1))
                    for g in range(GP):
                        ins = nc.tensor.matmul(ps[32 * g:32 * g + 32, 6 + s, :], Pw[:, s, GP * sl + g, :], values_in[s][:, sl, g, :],
                                               start=sl == 0, stop=sl == SLOTS - 1 and g > 0)
                    if sl == SLOTS - 1:
                        ins = nc.tensor.matmul(ps[0:32, 6 + s, :], Pw[0:NS, s, NPAGE, :], srows[0:NS, DA:2 * DA],
                                               start=False, stop=True)
                    ins.then_inc(s_vused, 1)

            def head_scores(i):
                pe.wait_ge(s_stg, 3 * i + 3)
                for s in range(2):
                    h = slice(64 * s, 64 * s + 64)
                    nc.tensor.matmul(ps[:, 4 + s, 0:P], stage[h, 0, 0:P], stage[h, 1, 0:P], start=True, stop=True)
                    nc.tensor.matmul(ps[:, 4 + s, P:3 * P], stage[h, 0, P:NPR], stage[h, 1, :], start=True, stop=True)\
                        .then_inc(s_sc, 1)

            def outputs(i):
                for s in range(2):
                    pe.wait_ge(s_hp, 2 * i + (s + 1))
                    for n in range(3):
                        ins = turn(ps[:, 1 + s, n * P:(n + 1) * P], hs[:, s, n * P:(n + 1) * P])
                    ins.then_inc(s_htp, 1)
                for s in range(2):
                    pe.wait_ge(s_ht, 2 * i + (s + 1))
                    out = ps[64 * s:64 * s + 64, 3, 0:NPR]
                    v = [vstage[:, r, 64 * s:64 * s + 64] for r in range(2)]
                    nc.tensor.matmul(out, v[0], hT[:, s, 0:NPR], start=True, stop=False)
                    nc.tensor.matmul(out[:, P:NPR], v[1], hT[:, s, NPR:3 * P], start=False, stop=True).then_inc(s_ho, 1)
                pe.wait_ge(s_otc, i + 1)
                for s in range(2):
                    pe.wait_ge(s_om, 2 * i + (s + 1 + 2))
                    for t in range(4):
                        ins = nc.tensor.matmul(ps[:, 0, 2 * t + s:2 * t + s + 1], OM[:, s, t * P:(t + 1) * P], ones[:, 0:1],
                                               start=True, stop=True)
                ins.then_inc(s_ot, 1)

            values(0, 0)
            values(0, 1)
            softmax_sums(1)
            pe.wait_ge(s_soft, 2)
            head_scores(0)
            outputs(0)
            with pe.Fori(1, 4) as i:
                values(i, 0)
                pe.wait_ge(s_scm, 2 * i)
                head_scores(i)
                values(i, 1)
                pe.wait_ge(s_hoc, i)
                outputs(i)

            pe.wait_ge(s_wo, 16)
            pe.wait_ge(s_cvT, 4)
            pe.wait_ge(s_otc, 5)
            for m in range(KT):
                if m >= 4:
                    pe.wait_ge(s_r1, m - 3)
                product(ps[:, m % 4, 0:R], [wr_out[:, k, m * P:(m + 1) * P] for k in range(KT)],
                        [catT[:, k, :] for k in range(KT)]).then_inc(s_mix, 1)

            def to_rows(done):
                for bank, c0, n in ((4, 0, P), (6, P, P), (2, NPR, NS)):
                    for m in range(KT):
                        ins = turn(ps[0:n, bank + m // 4, m % 4 * P:(m % 4 + 1) * P], rT[:, m, c0:c0 + n])
                    ins.then_inc(done, 1)

            pe.wait_ge(s_r1, KT)
            to_rows(s_n1)
            for r in range(3):
                pe.wait_ge(s_xh1, r + 1)
            for m in range(KT):
                if m >= 4:
                    pe.wait_ge(s_x1, m - 3)
                for r in range(2):
                    turn(ps[:, 4 + m % 4, r * P:(r + 1) * P], rows[:, r, m * P:(m + 1) * P])
                turn(ps[:, 4 + m % 4, NPR:R], srows[0:NS, m * P:(m + 1) * P], NS).then_inc(s_b1, 1)

            def split_product(out, wh, wl, xh, xl, ready=None, credits=0):
                n = len(wh)
                for k in range(n):
                    if ready is not None:
                        pe.wait_ge(ready, k + 1 + credits)
                    nc.tensor.matmul(out, wh[k], xh[k], start=k == 0, stop=False)
                    nc.tensor.matmul(out, wh[k], xl[k], start=False, stop=False)
                    ins = nc.tensor.matmul(out, wl[k], xh[k], start=False, stop=k == n - 1)
                return ins

            def up_tiles(u, s, first=False):
                wh, wl = (w[s][:, 0:KT * 2 * P].rearrange("p (k a n) -> p k a n", k=KT, a=2) for w in (whi, wlo))
                pe.wait_ge(s_lo, u + 1)
                for a in range(2):
                    pe.wait_ge(s_uz, 2 * u + (a + 1))
                    split_product(ps[:, 2 * s + a, 0:R], [wh[:, k, a, :] for k in range(KT)],
                                  [wl[:, k, a, :] for k in range(KT)], [x1h[:, k, :] for k in range(KT)],
                                  [x1l[:, k, :] for k in range(KT)], s_x1l if first and a == 0 else None).then_inc(s_u, 1)

            up_tiles(0, 0, first=True)
            up_tiles(1, 1)
            with pe.Fori(1, FT // 2) as j:
                for s in range(2):
                    up_tiles(2 * j + s, s)
            def down_tile(m, s, ready=None, credits=0):
                wh, wl = (w[s].rearrange("p (k n) -> p k n", k=FT) for w in (whi, wlo))
                pe.wait_ge(s_lo, m + (FT + 1))
                pe.wait_ge(s_r2, m + 1)
                split_product(ps[:, s, 0:R], [wh[:, k, :] for k in range(FT)], [wl[:, k, :] for k in range(FT)],
                              [fh[:, k, :] for k in range(FT)], [fl[:, k, :] for k in range(FT)], ready, credits)\
                    .then_inc(s_dn, 1)

            pe.wait_ge(s_uz, 4 + 2 * FT)
            down_tile(0, 0, s_fs, 2)
            for r in range(NTAIL):
                ins = turn(ps[0:2 * FT, 4 + r // 4, r % 4 * P:(r % 4 + 1) * P], uptail[:, r, :])
                if r % 4 == 3 or r == NTAIL - 1:
                    ins.then_inc(s_utps, 1)
            down_tile(1, 1)
            with pe.Fori(1, KT // 2) as j:
                for s in range(2):
                    down_tile(2 * j + s, s)
            pe.wait_ge(s_r2, 2 + KT)
            pe.wait_ge(s_ut, 3)
            to_rows(s_n2)


def constants():
    h = np.arange(1, NH + 1, dtype=np.float64)
    sl = (-8.0 * 2.0 ** (-8.0 * h / NH)).astype(np.float32)
    tok = np.arange(P)
    past = PAST - (np.arange(NPAGE)[None, :] * PAGE + tok[:, None])
    k = np.arange(P)
    d00 = tok[:, None] - k[None, :]
    own = np.where(d00 >= 0, d00, FAR)
    diag = np.zeros((P, NH, DH), np.float32)
    for c in range(4):
        for i in range(NH):
            diag[32 * c + i, i] = 1.0
    tie = np.arange(NBLK)[None, :] < np.arange(NBLK)[:, None]
    pick = tok[:, None] % 32 == np.arange(NS)[None, :]
    head = (tok[:, None] // DH == np.arange(2)[None, :])
    return {
        "c_ident": np.eye(P, dtype=np.float32),
        "c_dist": np.concatenate([own, d00 + P, own], 1).astype(np.float32),
        "c_bias": (past[:, :, None] * sl[None, None, :]).astype(np.float32),
        "c_slope": np.ascontiguousarray(np.broadcast_to(sl, (P, NH))),
        "c_diag": diag.reshape(P, DA),
        "c_head": head.astype(np.float32),
        "c_tie": np.ascontiguousarray(np.broadcast_to(tie, (P, NBLK, NBLK)).astype(np.int32)),
        "c_sel": pick.astype(np.float32),
    }


_INS = ["x_prompt", "x_sample", "cache_k", "cache_v", "state_conv", "state_ffn_conv", "page_table",
        "w_in", "w_conv", "w_out", "ln1_g", "ln1_b", "w_ffn_up", "w_ffn_conv", "w_ffn_down", "ln2_g", "ln2_b"]
_OUTS = [(1, NPR, D), (NS, 1, D), (1, 1, NPR, NH, DH), (1, 1, NPR, NH, DH), (1, 1, 2, DA), (1, 1, 2, 2 * FF),
         (1, NS, 1, NH, DH), (1, NS, 1, NH, DH), (1, NS, 2, DA), (1, NS, 2, 2 * FF)]


def kernel(**inputs):
    import concourse.bacc as _bacc
    from concourse.bass_utils import run_bass_kernel_spmd as _run

    nc = _bacc.Bacc("TRN2", target_bir_lowering=False, num_devices=1)
    given = {n: np.ascontiguousarray(inputs[n]) for n in _INS}
    given.update(constants())
    arrays, args = {}, []
    for name, a in given.items():
        arrays[f"in_{name}"] = a
        args.append(nc.dram_tensor(f"in_{name}", a.shape, mybir.dt.from_np(a.dtype), kind="ExternalInput").ap())
    for i, shape in enumerate(_OUTS):
        args.append(nc.dram_tensor(f"out_{i}", shape, F32, kind="ExternalOutput").ap())
    build(nc, *args)
    r = _run(nc, [arrays], core_ids=[0])
    return tuple(r.results[0][f"out_{i}"] for i in range(len(_OUTS)))
```
